# Optimizing a Trainium2 kernel written in Bass

```python
import numpy as np
import jax, jax.numpy as jnp
from jax import lax

D_MODEL = 1024
BATCH = 1
SEQ = 512
DEPTH = 2

HEAD_DIM = 64
ROPE_THETA = 10000.0
RMS_EPS = 1e-6
Q_BLOCK = 128
NEG_INF = -1e30
FORCE = 1e30

POOL_WINDOWS = (2, 4, 8, 16)
POOL_GROUPS = len(POOL_WINDOWS)
POOL_GROUP_DIM = D_MODEL // 16
POOL_DIM = POOL_GROUPS * POOL_GROUP_DIM
POOL_MAXW = max(POOL_WINDOWS)

NSA_HEADS = D_MODEL // 128
NSA_KV_GROUPS = 2
NSA_HPG = NSA_HEADS // NSA_KV_GROUPS
NSA_DIM = NSA_HEADS * HEAD_DIM
NSA_KV_DIM = NSA_KV_GROUPS * HEAD_DIM
CMP_BLOCK = 32
CMP_STRIDE = 16
CMP_HIDDEN = 256
SEL_BLOCK = 64
SEL_COUNT = 16
WINDOW = 512

MOBA_HEADS = 4
MOBA_DIM = MOBA_HEADS * HEAD_DIM
MOBA_BLOCK = 256
MOBA_TOPK = 3

D_FF = ((8 * D_MODEL + 3 * 256 - 1) // (3 * 256)) * 256

IN_SIZES = (POOL_DIM, NSA_DIM, 6 * NSA_KV_DIM, 3 * NSA_HEADS, 3 * MOBA_DIM, 3 * D_MODEL)
IN_COLS = sum(IN_SIZES)

kernel_name = "hybrid_pool_nsa_moba_block"

def rms_norm(x, g):
    xf = x.astype(jnp.float32)
    y = xf * lax.rsqrt(jnp.mean(xf * xf, axis=-1, keepdims=True) + RMS_EPS)
    return (y * g.astype(jnp.float32)).astype(x.dtype)

def rope_tables(seq):
    pos = jnp.arange(seq, dtype=jnp.float32)
    inv_freq = ROPE_THETA ** (-jnp.arange(0, HEAD_DIM, 2, dtype=jnp.float32) / HEAD_DIM)
    ang = pos[:, None] * inv_freq[None, :]
    return jnp.cos(ang), jnp.sin(ang)

def apply_rope(x, cos, sin):
    half = HEAD_DIM // 2
    x1, x2 = x[..., :half], x[..., half:]
    c = cos[:, None, :].astype(x.dtype)
    s = sin[:, None, :].astype(x.dtype)
    return jnp.concatenate([x1 * c - x2 * s, x2 * c + x1 * s], axis=-1)

def masked_softmax(scores, mask):
    s = jnp.where(mask, scores.astype(jnp.float32), NEG_INF)
    m = jnp.max(s, axis=-1, keepdims=True)
    p = jnp.exp(s - m) * mask
    return p / jnp.maximum(jnp.sum(p, axis=-1, keepdims=True), 1e-30)

def pool_mixer(u, pool_w, pool_scale):
    B, S, C = u.shape
    uf = u.astype(jnp.float32)
    csum = jnp.concatenate([jnp.zeros((B, POOL_MAXW, C), jnp.float32), jnp.cumsum(uf, axis=1)], axis=1)
    t = jnp.arange(S)
    pooled = []
    for gi, w in enumerate(POOL_WINDOWS):
        sl = slice(gi * POOL_GROUP_DIM, (gi + 1) * POOL_GROUP_DIM)
        total = csum[:, POOL_MAXW:POOL_MAXW + S, sl] - csum[:, POOL_MAXW - w:POOL_MAXW - w + S, sl]
        count = jnp.minimum(t + 1, w).astype(jnp.float32)
        pooled.append(total / count[None, :, None])
    d = jnp.concatenate(pooled, axis=-1) - uf
    d = d.reshape(B, S, POOL_GROUPS, POOL_GROUP_DIM)
    y = jnp.einsum("bsgc,gce->bsge", d, pool_w.astype(jnp.float32)).reshape(B, S, C)
    return (y * pool_scale.astype(jnp.float32)).astype(u.dtype)

def nsa_compress(kv, pos_emb, w1, b1, w2, b2):
    B, S, G, D = kv.shape
    n_cmp = (S - CMP_BLOCK) // CMP_STRIDE + 1
    idx = jnp.arange(n_cmp)[:, None] * CMP_STRIDE + jnp.arange(CMP_BLOCK)[None, :]
    blocks = kv[:, idx] + pos_emb[:, None, :]
    flat = blocks.transpose(0, 1, 3, 2, 4).reshape(B, n_cmp, G, CMP_BLOCK * D)
    hid = jax.nn.gelu(flat @ w1 + b1)
    return hid @ w2 + b2

def nsa_mixer(q, k_cmp, v_cmp, k_sel, v_sel, k_win, v_win, gate_logits, cmp_pos, cmp_w1, cmp_b1, cmp_w2, cmp_b2):
    B, S = q.shape[0], q.shape[1]
    G, Hg, D = NSA_KV_GROUPS, NSA_HPG, HEAD_DIM
    scale = HEAD_DIM ** -0.5
    qg = q.reshape(B, S, G, Hg, D)
    kc = nsa_compress(k_cmp, cmp_pos[0], cmp_w1[0], cmp_b1[0], cmp_w2[0], cmp_b2[0])
    vc = nsa_compress(v_cmp, cmp_pos[1], cmp_w1[1], cmp_b1[1], cmp_w2[1], cmp_b2[1])
    n_cmp = kc.shape[1]
    n_sel = S // SEL_BLOCK
    n_top = min(SEL_COUNT, n_sel)
    ratio = SEL_BLOCK // CMP_STRIDE
    overlap = CMP_BLOCK // CMP_STRIDE
    agg_w = np.convolve(np.ones(ratio), np.ones(overlap))
    pad_front = overlap - 1
    pad_back = ratio * n_sel + len(agg_w) - 1 - pad_front - n_cmp
    cmp_end = jnp.arange(n_cmp) * CMP_STRIDE + CMP_BLOCK - 1
    k_sel_blk = k_sel.transpose(0, 2, 1, 3).reshape(B, G, n_sel, SEL_BLOCK, D)
    v_sel_blk = v_sel.transpose(0, 2, 1, 3).reshape(B, G, n_sel, SEL_BLOCK, D)
    k_win_pad = jnp.pad(k_win, ((0, 0), (WINDOW, 0), (0, 0), (0, 0)))
    v_win_pad = jnp.pad(v_win, ((0, 0), (WINDOW, 0), (0, 0), (0, 0)))
    b_idx = jnp.arange(B)[:, None, None, None]
    g_idx = jnp.arange(G)[None, :, None, None]
    blk = jnp.arange(n_sel)

    def chunk(c):
        q0 = c * Q_BLOCK
        tq = q0 + jnp.arange(Q_BLOCK)
        qc = lax.dynamic_slice_in_dim(qg, q0, Q_BLOCK, axis=1)
        s_cmp = jnp.einsum("bqghd,bngd->bghqn", qc, kc) * scale
        p_cmp = masked_softmax(s_cmp, cmp_end[None, :] <= tq[:, None])
        o_cmp = jnp.einsum("bghqn,bngd->bqghd", p_cmp.astype(vc.dtype), vc)
        p_grp = jnp.sum(p_cmp, axis=2)
        p_pad = jnp.pad(p_grp, ((0, 0), (0, 0), (0, 0), (pad_front, pad_back)))
        p_slc = sum(float(agg_w[w]) * p_pad[..., w:w + ratio * n_sel:ratio] for w in range(len(agg_w)))
        cur = tq // SEL_BLOCK
        started = blk[None, :] <= cur[:, None]
        forced = (blk[None, :] == 0) | (blk[None, :] == cur[:, None]) | (blk[None, :] == cur[:, None] - 1)
        s_slc = jnp.where(forced, FORCE, jnp.where(started, p_slc, NEG_INF))
        _, sel = lax.top_k(s_slc, n_top)
        kb = k_sel_blk[b_idx, g_idx, sel].reshape(B, G, Q_BLOCK, n_top * SEL_BLOCK, D)
        vb = v_sel_blk[b_idx, g_idx, sel].reshape(B, G, Q_BLOCK, n_top * SEL_BLOCK, D)
        kpos = (sel[..., None] * SEL_BLOCK + jnp.arange(SEL_BLOCK)).reshape(B, G, Q_BLOCK, n_top * SEL_BLOCK)
        m_sel = (kpos <= tq[:, None])[:, :, None]
        s_sel = jnp.einsum("bqghd,bgqnd->bghqn", qc, kb) * scale
        p_sel = masked_softmax(s_sel, m_sel)
        o_sel = jnp.einsum("bghqn,bgqnd->bqghd", p_sel.astype(vb.dtype), vb)
        kw = lax.dynamic_slice_in_dim(k_win_pad, q0, Q_BLOCK + WINDOW, axis=1)
        vw = lax.dynamic_slice_in_dim(v_win_pad, q0, Q_BLOCK + WINDOW, axis=1)
        kpos_w = q0 - WINDOW + jnp.arange(Q_BLOCK + WINDOW)
        m_win = (kpos_w[None, :] <= tq[:, None]) & (kpos_w[None, :] > tq[:, None] - WINDOW) & (kpos_w[None, :] >= 0)
        s_win = jnp.einsum("bqghd,bkgd->bghqk", qc, kw) * scale
        p_win = masked_softmax(s_win, m_win)
        o_win = jnp.einsum("bghqk,bkgd->bqghd", p_win.astype(vw.dtype), vw)
        return o_cmp, o_sel, o_win

    o_cmp, o_sel, o_win = lax.map(chunk, jnp.arange(S // Q_BLOCK))

    def unchunk(y):
        return jnp.moveaxis(y, 0, 1).reshape(B, S, NSA_HEADS, D)

    g = jax.nn.sigmoid(gate_logits)
    out = g[..., 0:1] * unchunk(o_cmp) + g[..., 1:2] * unchunk(o_sel) + g[..., 2:3] * unchunk(o_win)
    return out.reshape(B, S, NSA_DIM)

def moba_mixer(q, k, v):
    B, S, H, D = q.shape
    scale = HEAD_DIM ** -0.5
    n_blk = -(-S // MOBA_BLOCK)
    s_pad = n_blk * MOBA_BLOCK - S
    k_pad = jnp.pad(k, ((0, 0), (0, s_pad), (0, 0), (0, 0)))
    v_pad = jnp.pad(v, ((0, 0), (0, s_pad), (0, 0), (0, 0)))
    k_blk = k_pad.reshape(B, n_blk, MOBA_BLOCK, H, D).transpose(0, 3, 1, 2, 4)
    v_blk = v_pad.reshape(B, n_blk, MOBA_BLOCK, H, D).transpose(0, 3, 1, 2, 4)
    k_mean = jnp.mean(k_blk.astype(jnp.float32), axis=3).astype(k.dtype)
    n_top = max(1, min(MOBA_TOPK, n_blk - 1))
    b_idx = jnp.arange(B)[:, None, None, None]
    h_idx = jnp.arange(H)[None, :, None, None]
    blk = jnp.arange(n_blk)

    def chunk(c):
        q0 = c * Q_BLOCK
        tq = q0 + jnp.arange(Q_BLOCK)
        own = q0 // MOBA_BLOCK
        qc = lax.dynamic_slice_in_dim(q, q0, Q_BLOCK, axis=1)
        s_gate = jnp.einsum("bqhd,bhnd->bhqn", qc, k_mean).astype(jnp.float32)
        s_gate = jnp.where(blk < own, s_gate, NEG_INF)
        _, sel = lax.top_k(s_gate, n_top)
        sel_ok = sel < own
        kb = k_blk[b_idx, h_idx, sel].reshape(B, H, Q_BLOCK, n_top * MOBA_BLOCK, D)
        vb = v_blk[b_idx, h_idx, sel].reshape(B, H, Q_BLOCK, n_top * MOBA_BLOCK, D)
        s_sel = jnp.einsum("bqhd,bhqnd->bhqn", qc, kb) * scale
        m_sel = jnp.repeat(sel_ok, MOBA_BLOCK, axis=-1)
        ko = lax.dynamic_slice_in_dim(k_pad, own * MOBA_BLOCK, MOBA_BLOCK, axis=1)
        vo = lax.dynamic_slice_in_dim(v_pad, own * MOBA_BLOCK, MOBA_BLOCK, axis=1)
        s_own = jnp.einsum("bqhd,bkhd->bhqk", qc, ko) * scale
        kpos = own * MOBA_BLOCK + jnp.arange(MOBA_BLOCK)
        m_own = jnp.broadcast_to(kpos[None, :] <= tq[:, None], (B, H, Q_BLOCK, MOBA_BLOCK))
        p = masked_softmax(jnp.concatenate([s_sel, s_own], axis=-1),
                           jnp.concatenate([m_sel, m_own], axis=-1)).astype(v.dtype)
        n_s = n_top * MOBA_BLOCK
        return (jnp.einsum("bhqn,bhqnd->bqhd", p[..., :n_s], vb)
                + jnp.einsum("bhqk,bkhd->bqhd", p[..., n_s:], vo))

    out = lax.map(chunk, jnp.arange(S // Q_BLOCK))
    return jnp.moveaxis(out, 0, 1).reshape(B, S, H * D)

def setup_inputs(seed: int = 0) -> dict:
    key = jax.random.key(seed)
    ks = jax.random.split(key, 20)
    f32 = jnp.float32

    def nrm(k, shape, s):
        return jax.random.normal(k, shape, f32) * s

    return {
        "x": nrm(ks[0], (BATCH, SEQ, D_MODEL), 1.0),
        "attn_norm": 1.0 + nrm(ks[1], (DEPTH, D_MODEL), 0.05),
        "w_in": nrm(ks[2], (DEPTH, D_MODEL, IN_COLS), D_MODEL ** -0.5),
        "b_in": nrm(ks[3], (DEPTH, IN_COLS), 0.02),
        "pool_w": nrm(ks[4], (DEPTH, POOL_GROUPS, POOL_GROUP_DIM, POOL_GROUP_DIM), POOL_GROUP_DIM ** -0.5),
        "pool_scale": 1.0 + nrm(ks[5], (DEPTH, POOL_DIM), 0.05),
        "cmp_pos": nrm(ks[6], (DEPTH, 2, CMP_BLOCK, HEAD_DIM), 0.1),
        "cmp_w1": nrm(ks[7], (DEPTH, 2, CMP_BLOCK * HEAD_DIM, CMP_HIDDEN), (CMP_BLOCK * HEAD_DIM) ** -0.5),
        "cmp_b1": nrm(ks[8], (DEPTH, 2, CMP_HIDDEN), 0.02),
        "cmp_w2": nrm(ks[9], (DEPTH, 2, CMP_HIDDEN, HEAD_DIM), CMP_HIDDEN ** -0.5),
        "cmp_b2": nrm(ks[10], (DEPTH, 2, HEAD_DIM), 0.02),
        "w_br_pool": nrm(ks[11], (DEPTH, POOL_DIM, D_MODEL), POOL_DIM ** -0.5),
        "w_br_nsa": nrm(ks[12], (DEPTH, NSA_DIM, D_MODEL), NSA_DIM ** -0.5),
        "w_br_moba": nrm(ks[13], (DEPTH, MOBA_DIM, D_MODEL), MOBA_DIM ** -0.5),
        "w_out": nrm(ks[14], (DEPTH, D_MODEL, D_MODEL), D_MODEL ** -0.5),
        "ffn_norm": 1.0 + nrm(ks[15], (DEPTH, D_MODEL), 0.05),
        "w_gate": nrm(ks[16], (DEPTH, D_MODEL, D_FF), D_MODEL ** -0.5),
        "w_up": nrm(ks[17], (DEPTH, D_MODEL, D_FF), D_MODEL ** -0.5),
        "w_down": nrm(ks[18], (DEPTH, D_FF, D_MODEL), D_FF ** -0.5),
        "final_norm": 1.0 + nrm(ks[19], (D_MODEL,), 0.05),
    }

def reference(x, attn_norm, w_in, b_in, pool_w, pool_scale, cmp_pos, cmp_w1, cmp_b1, cmp_w2, cmp_b2,
              w_br_pool, w_br_nsa, w_br_moba, w_out, ffn_norm, w_gate, w_up, w_down, final_norm):
    B, S, _ = x.shape
    cos, sin = rope_tables(S)
    split_at = np.cumsum(IN_SIZES)[:-1].tolist()
    for l in range(DEPTH):
        h = rms_norm(x, attn_norm[l])
        proj = h @ w_in[l] + b_in[l]
        u_pool, q_nsa, kv_nsa, g_nsa, qkv_moba, g_br = jnp.split(proj, split_at, axis=-1)

        a = pool_mixer(u_pool, pool_w[l], pool_scale[l])

        q_n = apply_rope(q_nsa.reshape(B, S, NSA_HEADS, HEAD_DIM), cos, sin)
        kv = kv_nsa.reshape(B, S, 6, NSA_KV_GROUPS, HEAD_DIM)
        k_c = apply_rope(kv[:, :, 0], cos, sin)
        k_s = apply_rope(kv[:, :, 2], cos, sin)
        k_w = apply_rope(kv[:, :, 4], cos, sin)
        b = nsa_mixer(q_n, k_c, kv[:, :, 1], k_s, kv[:, :, 3], k_w, kv[:, :, 5],
                      g_nsa.reshape(B, S, NSA_HEADS, 3),
                      cmp_pos[l], cmp_w1[l], cmp_b1[l], cmp_w2[l], cmp_b2[l])

        qkv = qkv_moba.reshape(B, S, 3, MOBA_HEADS, HEAD_DIM)
        c = moba_mixer(apply_rope(qkv[:, :, 0], cos, sin), apply_rope(qkv[:, :, 1], cos, sin),
                       qkv[:, :, 2])

        gate = jax.nn.sigmoid(g_br)
        g_a, g_b, g_c = jnp.split(gate, 3, axis=-1)
        merged = g_a * (a @ w_br_pool[l]) + g_b * (b @ w_br_nsa[l]) + g_c * (c @ w_br_moba[l])
        x = x + merged @ w_out[l]

        h2 = rms_norm(x, ffn_norm[l])
        x = x + (jax.nn.silu(h2 @ w_gate[l]) * (h2 @ w_up[l])) @ w_down[l]
    return rms_norm(x, final_norm)


_drawn_inputs = setup_inputs


def setup_inputs(seed=0):
    import zlib

    import numpy as np

    out = dict(_drawn_inputs(seed))
    spreads = {}
    factors = {'cmp_pos': 2.688, 'cmp_b1': 8.0, 'cmp_b2': 7.329}
    for name, (base, spread) in spreads.items():
        noise = np.random.default_rng([zlib.crc32(name.encode()), seed]).standard_normal(out[name].shape)
        drawn = base * np.exp(spread * noise) if base else spread * noise
        out[name] = __import__('jax').numpy.asarray(drawn.astype(out[name].dtype))
    for name, factor in factors.items():
        out[name] = (out[name] * factor).astype(out[name].dtype)
    return out
```

```python
from contextlib import ExitStack

import concourse.bass as bass
from concourse import mybir

ALU = mybir.AluOpType
ACT = mybir.ActivationFunctionType
AX = mybir.AxisListType
F32 = mybir.dt.float32
F32R = mybir.dt.float32r
BF16 = mybir.dt.bfloat16
ds = bass.ds

P = 128
D = 1024
S = 512
LAYERS = 2
DK = D // P
QT = S // P
HD = 64
FF = 2816
FT = FF // P
EPS = 1e-6
NEG = -1e30
QSCALE = HD ** -0.5
CMP_STRIDE = 16
NCMP = (S - 32) // CMP_STRIDE + 1
NC_PAD = 32
GELU_A = 0.044715
GELU_B = 0.7978845608028654

CH = 1024
RING = 4
C_F1, C_MIX, C_AT, C_BR, C_OUT, C_GU, C_DN, NCH = 0, 18, 30, 50, 58, 66, 110, 132
MIX = "kkGkkGvvGvvG"
MIX_G = MIX.count("G")
NLIN = 43
F1 = [(768, "kc", 0), (896, "vc", 0), (1024, "k", 0), (1280, "k", 1), (1816, "k", 2), (1944, "k", 3),
      (256, "q", 0), (384, "q", 1), (512, "q", 2), (640, "q", 3), (1560, "q", 4), (1688, "q", 5),
      (1152, "v", 0), (1408, "v", 1), (2072, "v", 2), (2200, "v", 3), (0, "u", 0), (128, "u", 1)]
ROPED = [c for c, t in enumerate(F1) if t[1] in ("kc", "k", "q")]
VTILES = [c for c, t in enumerate(F1) if t[1] == "v"]
NG_COL, NG, GT_W = 1536, 24, 32
BG_COL = 2328

V_AN, V_B1N, V_BNG, V_BG, V_PS, V_FN, V_CB1, V_CB2, V_POS, V_CB2V, NV = 0, 8, 26, 27, 51, 53, 61, 65, 66, 98, 162
W_NG, W_2K, W_2V, W_PW, NSW = 0, 192, 448, 576, 832
K_ID, K_ONE, K_COS, K_SIN, K_CM0, K_CM1, K_INV, K_INVW, NK = 0, 128, 256, 768, 1280, 1408, 1536, 1568, 1570


DVE_LINKS, POOL_LINKS = 62, 34


def trunk(nc, xT, weights, vectors, small, consts, causal, final_norm, out):
    KB = 1024
    base = 16640
    at = {}

    def place(name, shape, dt, offset):
        at[name] = offset
        return nc.alloc_sbuf_tensor_at(name, shape, dt, offset=base + offset)

    x = place("x", [P, DK, S], F32, 0)
    h_hi = place("h_hi", [P, DK, S], F32R, 16 * KB)
    h_lo = place("h_lo", [P, DK, S], F32R, 32 * KB)
    abc_hi = place("abc_hi", [P, DK, S], F32R, 16 * KB)
    abc_lo = place("abc_lo", [P, DK, S], F32R, 32 * KB)
    w_raw = place("w_raw", [P, RING, CH], F32, 48 * KB)
    w_rem = place("w_rem", [P, RING, CH], F32R, 48 * KB)
    w_top = place("w_top", [P, RING, CH], F32R, 64 * KB)
    act_hi = place("act_hi", [P, FT, S], F32R, 80 * KB)
    act_lo = place("act_lo", [P, FT, S], F32R, 124 * KB)
    gates = place("gates", [P, 24, S], F32, 80 * KB)
    mg_hi = place("mg_hi", [P, DK, S], F32R, 80 * KB)
    mg_lo = place("mg_lo", [P, DK, S], F32R, 96 * KB)
    sq = place("sq", [P, S], F32, 112 * KB)
    cmp_src = place("cmp_src", [P, 2, S], F32, 104 * KB)
    cmp_x = place("cmp_x", [P, 2, S], F32, 108 * KB)
    cmp_b = place("cmp_b", [P, 2, 16, 2 * NCMP], F32, 112 * KB)
    cmp_blo = place("cmp_blo", [P, 2, 16, 2 * NCMP], F32R, 112 * KB)
    cmp_bhi = place("cmp_bhi", [P, 2, 16, 2 * NCMP], F32R, 120 * KB)
    qs = place("qs", [P, 6, S], F32, 128 * KB)
    ks = place("ks", [P, 4, S], F32, 140 * KB)
    vs = place("vs", [P, QT, 4, P], F32, 148 * KB)
    o_all = qs
    pcT = place("pcT", [P, 2, S], F32, 112 * KB)
    o_cmp = place("o_cmp", [P, 4, S], F32, 120 * KB)
    probs = place("probs", [P, 2, S], F32, 156 * KB)
    pT = place("pT", [P, 2, QT, P], F32, 160 * KB)
    o_row = place("o_row", [P, 2, QT, P], F32, 180 * KB)
    pool_u = place("pool_u", [P, 16 + S], F32, 156 * KB)
    pool_b = place("pool_b", [P, 16 + S], F32, 156 * KB + 2112)
    pool_c = place("pool_c", [P, 16 + S], F32, 156 * KB + 4224)
    cmp_s = place("cmp_s", [P, QT, 8, NC_PAD], F32, 156 * KB)
    cmp_p = place("cmp_p", [P, QT, 8, NC_PAD], F32, 160 * KB)
    pool_d = place("pool_d", [P, 2, S], F32, 164 * KB)
    a_out = pool_d
    r_in = place("r_in", [P, 2, S], F32, 168 * KB)
    r_sw = place("r_sw", [P, 2, S], F32, 172 * KB)
    r_m = place("r_m", [P, 2, S], F32, 176 * KB)
    vt = place("vt", [P, 2, S], F32, 180 * KB)
    hid = place("hid", [P, 6, 2 * 2 * NCMP], F32, 96 * KB)
    ng_sig = place("ng_sig", [P, S], F32, 100 * KB)
    st_q = place("st_q", [P, 2, S], F32, 168 * KB)
    st_k = place("st_k", [P, 2, S], F32, 172 * KB)
    st_v = place("st_v", [P, 2, QT, P], F32, 176 * KB)
    br_t = place("br_t", [P, 6, S], F32, 168 * KB)
    br_m = place("br_m", [P, 2, S], F32, 180 * KB)
    f_g = place("f_g", [P, 2, S], F32, 168 * KB)
    f_s = place("f_s", [P, 2, S], F32, 172 * KB)
    f_u = place("f_u", [P, 2, S], F32, 176 * KB)
    f_a = place("f_a", [P, 2, S], F32, 180 * KB)
    rstd = place("rstd", [P, S], F32, 184 * KB)
    ssq = place("ssq", [P, S], F32, 186 * KB)
    tmp = place("tmp", [P, 2, S], F32, 188 * KB)
    kon = place("kon", [P, NK], F32, 192 * KB)
    o = 192 * KB + 4 * 1576
    vec = place("vec", [P, NV], F32, o); o += 4 * 168
    sw = place("sw", [P, NSW], F32, o); o += 4 * NSW
    ng_hi = place("ng_hi", [P, DK * NG], F32R, o); o += 4 * 192
    ng_lo = place("ng_lo", [P, DK * NG], F32R, o); o += 4 * 192
    k16 = place("k16", [P, 2, P], BF16, o); o += 512
    gt = place("gt", [P, QT, GT_W], F32, o); o += 4 * QT * GT_W
    kcmp = place("kcmp", [P, 2, NC_PAD], F32, o); o += 256
    vcmp = place("vcmp", [P, 2, P], F32, o); o += 1024
    st_c = place("st_c", [P, 4, 32], F32, o); o += 512
    row_max = place("row_max", [P, 2], F32, o); o += 32
    row_sum = place("row_sum", [P, 4, 3, QT], F32, o); o += 192
    qb = place("qb", [P, 8], F32, o); o += 32
    gb = place("gb", [P, 26], F32, o); o += 128
    epsb = place("epsb", [P, 8], F32, o); o += 32
    fn = place("fn", [P, 8], F32, o); o += 32
    o_end = base + o

    ident = kon[:, K_ID:K_ID + P]
    ones = kon[:, K_ONE:K_ONE + P]
    cos = kon[:, K_COS:K_COS + S]
    sin = kon[:, K_SIN:K_SIN + S]
    cm_neg = kon[:, K_CM0:K_CM0 + QT * NC_PAD].rearrange("p (q n) -> p q n", q=QT)
    cm_one = kon[:, K_CM1:K_CM1 + QT * NC_PAD].rearrange("p (q n) -> p q n", q=QT)
    assert o_end <= nc.sbuf_usable_end, o_end - nc.sbuf_usable_end

    with ExitStack() as ctx:
        def sem(name):
            return ctx.enter_context(nc.semaphore(name))

        bank = [ctx.enter_context(nc.psum_tensor(f"bank{b}", [P, S], F32)) for b in range(8)]

        const_in = sem("const_in")
        small_in = sem("small_in")
        raw_in = [sem(f"raw_in{s}") for s in range(RING)]
        w_split_hi = sem("w_split_hi")
        w_ready = sem("w_ready")
        w_used = sem("w_used")
        x_ready = sem("x_ready")
        xg_done = sem("xg_done")
        h_ready = sem("h_ready")
        ssq_ready = sem("ssq_ready")
        ms_done = sem("ms_done")
        std_done = sem("std_done")
        rstd_done = sem("rstd_done")
        ng_done = sem("ng_done")
        lin_evac = sem("lin_evac")
        y_done = sem("y_done")
        r_swapped = [sem(f"r_swapped{s}") for s in range(2)]
        r_mul = sem("r_mul")
        roped = sem("roped")
        vt_done = sem("vt_done")
        v_ready = sem("v_ready")
        ng_split = sem("ng_split")
        ng_w = sem("ng_w")
        gb_done = sem("gb_done")
        qb_done = sem("qb_done")
        pool_sum = sem("pool_sum")
        d_ready = sem("d_ready")
        py_done = sem("py_done")
        a_ready = sem("a_ready")
        ngt_done = sem("ngt_done")
        gt_ready = sem("gt_ready")
        cx_in = sem("cx_in")
        cb_ready = sem("cb_ready")
        cb_hi = sem("cb_hi")
        cb_lo = sem("cb_lo")
        hid_done = sem("hid_done")
        gelu_t = sem("gelu_t")
        gelu_a = sem("gelu_a")
        gelu_done = sem("gelu_done")
        kc_done = sem("kc_done")
        kc_ready = sem("kc_ready")
        cs_done = sem("cs_done")
        cs_arg = sem("cs_arg")
        cs_exp = sem("cs_exp")
        cp_ready = sem("cp_ready")
        vc_done = sem("vc_done")
        vc_ready = sem("vc_ready")
        cpt_done = sem("cpt_done")
        cpt_ready = sem("cpt_ready")
        co_done = sem("co_done")
        co_ready = sem("co_ready")
        staged = [sem(f"staged{s}") for s in range(2)]
        at_s = sem("at_s")
        at_max = sem("at_max")
        at_exp = sem("at_exp")
        at_scale = sem("at_scale")
        at_t = sem("at_t")
        at_ca = sem("at_ca")
        at_cd = sem("at_cd")
        at_pv = sem("at_pv")
        ot_done = sem("ot_done")
        at_o = sem("at_o")
        abc_h = sem("abc_h")
        abc_ready = sem("abc_ready")
        br_done = sem("br_done")
        br_mul = sem("br_mul")
        br_sum = sem("br_sum")
        br_hi = sem("br_hi")
        m_ready = sem("m_ready")
        out_done = sem("out_done")
        gu_done = sem("gu_done")
        gu_evac = sem("gu_evac")
        silu_done = sem("silu_done")
        fa_ready = sem("fa_ready")
        fa_hi = sem("fa_hi")
        f_ready = sem("f_ready")
        dn_done = sem("dn_done")
        dve_chain = sem("dve_chain")
        act_chain = sem("act_chain")
        pool_self = sem("pool_self")
        br_part = sem("br_part")
        eps_set = sem("eps_set")
        passed = sem("passed")
        fin_done = sem("fin_done")
        stored = sem("stored")


        class Chain:

            def __init__(self, eng, s, l, per_layer):
                self.eng, self.s, self.base, self.k, self.per = eng, s, l * per_layer, 0, per_layer

            def link(self, ins):
                ins.then_inc(self.s, 1)
                self.k += 1
                self.eng.wait_ge(self.s, self.base + self.k)

            def enter(self, i, n, step, first=0):
                self.outer = (self.base, self.k, n, step, first)
                self.base = self.base + i * step
                self.k -= first * step

            def leave(self):
                base, k, n, step, first = self.outer
                assert self.k - k == step - first * step, (self.s, self.k - k)
                self.base, self.k = base, k + n * step

            def end(self):
                assert self.k == self.per, (self.s, self.k)

        def flat_rows(dram, i):
            return dram[ds(i, 1)].rearrange("a p n -> p (a n)")

        def settle(eng):
            eng.sem_inc(passed, 1)

        def flat(ap):
            return ap.rearrange("p a s -> p (a s)")

        block = ctx.enter_context(nc.Block())

        @block.sync
        def _(sp):
            sp.dma_start(x[:], xT).then_inc(const_in, 16)
            sp.dma_start(kon[:], consts).then_inc(const_in, 16)
            sp.dma_start(tmp[:, 0, 0:P], causal).then_inc(const_in, 16)
            sp.dma_start(fn[:], final_norm).then_inc(const_in, 16)
            with sp.Fori(0, LAYERS) as l:
                sp.wait_ge(h_ready, 16 * l + 1)
                sp.dma_start(vec[:], flat_rows(vectors, l)).then_inc(small_in, 16)
                sp.dma_start(sw[:], flat_rows(small, l)).then_inc(small_in, 16)

                def loads(first, n):
                    with sp.Fori(0, n // RING) as i:
                        for j in range(RING):
                            slot = (first + j) % RING
                            sp.wait_ge(w_used, NCH * l + RING * i + (first + j + 1))
                            sp.dma_start(w_raw[:, slot, :], flat_rows(weights, NCH * l + RING * i + (first + j))
                                         ).then_inc(raw_in[slot], 16)

                def stack_tokens(kv):
                    if kv == 0:
                        sp.wait_ge(roped, 11 * l + 1)
                    else:
                        sp.wait_ge(y_done, NLIN * l + 2)
                        sp.wait_ge(cb_ready, 2 * l + 1)
                    for g in range(2):
                        src = cmp_src[HD * g:HD * g + HD, kv, :]
                        sp.dma_start(cmp_x[0:HD, g, :], src).then_inc(cx_in, 16)
                        sp.dma_start(cmp_x[HD:P, g, 0:S - 1], src[:, 1:S]).then_inc(cx_in, 16)

                def load_one(c, i=None):
                    at_c = NCH * l + c if i is None else NCH * l + RING * i + c
                    sp.wait_ge(w_used, at_c + 1)
                    sp.dma_start(w_raw[:, c % RING, :], flat_rows(weights, at_c)).then_inc(raw_in[c % RING], 16)

                def stage(s, q_src, kv_tile, heads):
                    sp.dma_start(st_q[:, s, :], q_src).then_inc(staged[s], 16)
                    for half, g in enumerate(heads):
                        sp.dma_start(st_k[HD * half:HD * half + HD, s, :],
                                     ks[HD * g:HD * g + HD, kv_tile, :]).then_inc(staged[s], 16)
                        sp.dma_start(st_v[:, s, :, HD * half:HD * half + HD],
                                     vs[:, :, kv_tile, HD * g:HD * g + HD]).then_inc(staged[s], 16)

                def turn(i, q_srcs, kv_tiles, heads):
                    for j in range(RING):
                        load_one(C_AT + RING + j, i)
                        if j % 2:
                            s = j // 2
                            sp.wait_ge(at_pv, 80 * l + 16 * i + (8 * s + 8 + 2))
                            stage(s, q_srcs[s], kv_tiles[s], heads)

                loads(0, 16)
                stack_tokens(0)
                loads(16, 8)
                stack_tokens(1)
                loads(24, 8)
                sp.wait_ge(roped, 11 * l + 11)
                sp.wait_ge(v_ready, 4 * l + 4)
                for s in range(2):
                    stage(s, qs[:, 0, :], s, (0, 0))
                load_one(32)
                load_one(33)
                for g, turns in ((0, (0, 1)), (1, (1, 3))):
                    with sp.Fori(*turns) as i:
                        q_src = flat(qs[:, ds(i + 1, 1), :])
                        turn(i, (q_src, q_src), (0, 1), (g, g))
                turn(3, (qs[:, 4, :], qs[:, 5, :]), (2, 3), (0, 1))
                for c in range(50, 56):
                    load_one(c)
                loads(56, 76)
            for n in range(DK):
                sp.wait_ge(fin_done, n + 1)
                sp.dma_start(out[:, n, :], x[:, n, :]).then_inc(stored, 16)
            sp.wait_ge(stored, 16 * DK)

        @block.tensor
        def _(pe):
            pe.sem_inc(w_used, RING)
            pe.sem_inc(ms_done, 1)
            pe.sem_inc(at_pv, 2)
            pe.sem_inc(at_t, 2)
            pe.wait_ge(eps_set, 6)
            pe.wait_ge(const_in, 64)

            def split_product(dst, top, rem, hi, lo, first, last, skip=False):
                nc.tensor.matmul(dst, top, hi, start=first, stop=False, skip_group_check=skip)
                nc.tensor.matmul(dst, rem, hi, start=False, stop=False, skip_group_check=skip)
                return nc.tensor.matmul(dst, top, lo, start=False, stop=last, skip_group_check=skip)

            def column_tile(slot, dst, hi, lo, k0=0, k1=DK, each=None):
                for k in range(k0, k1):
                    if each is not None:
                        each(k)
                    mm = split_product(dst, w_top[:, slot, k * P:k * P + P], w_rem[:, slot, k * P:k * P + P],
                                       hi[:, k, :], lo[:, k, :], k == k0, k == k1 - 1)
                return mm

            def sum_squares(count):
                pe.wait_ge(ssq_ready, count)
                nc.tensor.matmul(bank[7][:], ones, ssq[:], start=True, stop=True).then_inc(ms_done, 1)

            with pe.Fori(0, LAYERS) as l:
                def turn_v(n):
                    pe.wait_ge(y_done, NLIN * l + VTILES[n] + 1)
                    if n >= 2:
                        pe.wait_ge(v_ready, 4 * l + n - 1)
                    for t in range(QT):
                        mm = nc.tensor.transpose(bank[4 + n % 2][:, t * P:t * P + P],
                                                 vt[:, n % 2, t * P:t * P + P], ident)
                    mm.then_inc(vt_done, 1)

                for c in range(18):
                    pe.wait_ge(w_ready, NCH * l + c + 1)
                    if c >= 4:
                        pe.wait_ge(lin_evac, NLIN * l + c - 3)
                    each = (lambda k: pe.wait_ge(h_ready, 16 * l + k + 2)) if c == 0 else None
                    column_tile(c % RING, bank[c % 4][:], h_hi, h_lo, each=each).then_inc(w_used, 1)
                    if c == 0:
                        sum_squares(16 * l + 8)
                    if c - 2 in VTILES:
                        turn_v(VTILES.index(c - 2))
                pe.wait_ge(ng_split, l + 1)
                pe.wait_ge(lin_evac, NLIN * l + 15)
                for k in range(DK):
                    mm = split_product(bank[2][0:NG, :], ng_hi[:, k * NG:k * NG + NG], ng_lo[:, k * NG:k * NG + NG],
                                       h_hi[:, k, :], h_lo[:, k, :], k == 0, k == DK - 1)
                mm.then_inc(ng_done, 1)

                def hidden_chunk(c, kv, q):
                    pe.wait_ge(w_ready, NCH * l + c + 1)
                    for jj in range(4):
                        for m in range(2):
                            w0 = jj * 256 + m * P
                            mm = split_product(bank[7 - kv][:, m * 2 * NCMP:(m + 1) * 2 * NCMP],
                                               w_top[:, c % RING, w0:w0 + P], w_rem[:, c % RING, w0:w0 + P],
                                               cmp_bhi[:, kv, 4 * q + jj, :], cmp_blo[:, kv, 4 * q + jj, :],
                                               q == 0 and jj == 0 and m == 0, q == 3 and jj == 3, skip=True)
                    mm.then_inc(w_used, 1)

                gate_n, hidden_n = 0, 0
                for m, kind in enumerate(MIX):
                    c = C_MIX + m
                    if kind == "G":
                        pe.wait_ge(w_ready, NCH * l + c + 1)
                        pe.wait_ge(lin_evac, NLIN * l + 19 + gate_n - 3)
                        column_tile(c % RING, bank[(19 + gate_n) % 4][:], h_hi, h_lo).then_inc(w_used, 1)
                        gate_n += 1
                    else:
                        if hidden_n % 4 == 0:
                            pe.wait_ge(cb_lo, 2 * l + hidden_n // 4 + 1)
                            if kind == "v":
                                pe.wait_ge(gt_ready, l + 1)
                        hidden_chunk(c, hidden_n // 4, hidden_n % 4)
                        hidden_n += 1
                    if m == 2:
                        pe.wait_ge(d_ready, 2 * l + 2)
                        pe.wait_ge(v_ready, 4 * l + 4)
                        for t in range(2):
                            nc.tensor.matmul(bank[4 + t][:], sw[:, W_PW + t * P:W_PW + t * P + P], pool_d[:, t, :],
                                             start=True, stop=True).then_inc(py_done, 1)
                        pe.wait_ge(y_done, NLIN * l + 19)
                        settle(pe)
                        for t in range(QT):
                            mm = nc.tensor.transpose(bank[6][:, t * NG:t * NG + NG], ng_sig[0:NG, t * P:t * P + P],
                                                     ident[0:NG, 0:NG])
                        mm.then_inc(ngt_done, 1)
                    if m == 6:
                        pe.wait_ge(gelu_done, 2 * l + 1)
                        pe.wait_ge(a_ready, 2 * l + 2)
                        for half in range(2):
                            mm = nc.tensor.matmul(bank[4][:, 0:2 * NCMP], sw[:, W_2K + half * P:W_2K + half * P + P],
                                                  hid[:, 3, half * 2 * NCMP:(half + 1) * 2 * NCMP],
                                                  start=half == 0, stop=half == 1)
                        mm.then_inc(kc_done, 1)
                    if m == 8:
                        pe.wait_ge(kc_ready, l + 1)
                        pe.wait_ge(roped, 11 * l + 11)
                        for qt in range(QT):
                            for h in range(8):
                                half = HD * (h % 2)
                                col = (qt * 4 + h // 2) * NC_PAD
                                mm = nc.tensor.matmul(bank[5 - h % 2][:, col:col + NC_PAD],
                                                      qs[half:half + HD, h // 2, qt * P:qt * P + P],
                                                      kcmp[half:half + HD, h // 4, :], start=True, stop=True)
                        mm.then_inc(cs_done, 1)

                pe.wait_ge(gelu_done, 2 * l + 2)
                for g in range(2):
                    for a in range(4):
                        for m in range(2):
                            mm = nc.tensor.matmul(bank[6][32 * a:32 * a + NCMP, g * HD:g * HD + HD],
                                                  hid[:, 4, (m * 2 + g) * NCMP:(m * 2 + g + 1) * NCMP],
                                                  sw[:, W_2V + m * HD:W_2V + m * HD + HD], start=m == 0, stop=m == 1)
                mm.then_inc(vc_done, 1)
                pe.wait_ge(cp_ready, l + 1)
                for quad in range(2):
                    for qt in range(QT):
                        mm = nc.tensor.transpose(
                            bank[5 - quad][:, qt * P:qt * P + P],
                            cmp_p[:, qt, 4 * quad:4 * quad + 4, :].rearrange("p h n -> p (h n)"), ident)
                    mm.then_inc(cpt_done, 1)
                pe.wait_ge(vc_ready, l + 1)
                pe.wait_ge(cpt_ready, 2 * l + 2)
                pe.wait_ge(lin_evac, NLIN * l + 19 + MIX_G)
                for pair in range(4):
                    half = HD * (pair % 2)
                    mm = nc.tensor.matmul(bank[2 + pair][:], vcmp[half:half + HD, pair // 2, :],
                                          pcT[half:half + HD, pair // 2, :], start=True, stop=True)
                mm.then_inc(co_done, 1)


                def scores(i, t):
                    s, half, qt = t // 8, HD * (t // 4 % 2), t % 4
                    if t % 8 == 0:
                        pe.wait_ge(staged[s], 400 * l + 80 * i + 80)
                    pe.wait_ge(at_exp, 80 * l + 16 * i + (t + 1))
                    n = (qt + 1) * P
                    nc.tensor.matmul(bank[t % 2][:, 0:n], st_q[half:half + HD, s, qt * P:qt * P + P],
                                     st_k[half:half + HD, s, 0:n], start=True, stop=False)
                    nc.tensor.matmul(bank[t % 2][:, qt * P:n], k16[:, 0, :], k16[:, 1, :],
                                     start=False, stop=True).then_inc(at_s, 1)

                def turn_probs(i, t):
                    pe.wait_ge(at_exp, 80 * l + 16 * i + (t + 1 + 2))
                    pe.wait_ge(at_ca if t % 2 else at_cd, 40 * l + 8 * i + (t // 2 + 1))
                    for kt in range(t % 4 + 1):
                        mm = nc.tensor.transpose(bank[2 + t % 2][:, kt * P:kt * P + P],
                                                 probs[:, t % 2, kt * P:kt * P + P], ident)
                    mm.then_inc(at_t, 1)

                def tile_out(i, t, first=False, last=False):
                    h, qt = t // 4, t % 4
                    pe.wait_ge(at_ca if t % 2 else at_cd, 40 * l + 8 * i + (t // 2 + 2))
                    if qt == 0:
                        pe.wait_ge(at_scale, 20 * l + 4 * i + (h + 1))
                        if h == 1 and not first:
                            pe.wait_ge(at_o, 6 * l + i + 1)
                        if h == 3 and last:
                            pe.wait_ge(at_o, 6 * l + 6)
                    for kt in range(qt + 1):
                        mm = nc.tensor.matmul(bank[4 + h % 2][:, qt * HD:qt * HD + HD], pT[:, t % 2, kt, :],
                                              st_v[:, h // 2, kt, HD * (h % 2):HD * (h % 2) + HD],
                                              start=kt == 0, stop=kt == qt)
                    mm.then_inc(at_pv, 1)

                def pair_out(i, dst, branches):
                    pe.wait_ge(at_scale, 20 * l + 4 * i + (2 * branches[-1] + 2 + 2))
                    pe.wait_ge(at_o, 6 * l + i + 1)
                    for qt in range(QT):
                        for s in branches:
                            mm = nc.tensor.matmul(dst[:, qt * P:qt * P + P], o_row[:, s, qt, :], ident,
                                                  start=s == branches[0], stop=s == branches[-1])
                    mm.then_inc(ot_done, 1)

                def gate_steps(i, t):
                    j, k0 = t // 4, 2 * (t % 4)
                    c = C_AT + j
                    if k0 == 0:
                        pe.wait_ge(w_ready, NCH * l + RING * i + (c + 1))
                        pe.wait_ge(lin_evac, NLIN * l + RING * i + (19 + MIX_G + j - 1))
                    for k in (k0, k0 + 1):
                        mm = split_product(bank[6 + j % 2][:], w_top[:, c % RING, k * P:k * P + P],
                                           w_rem[:, c % RING, k * P:k * P + P], h_hi[:, k, :], h_lo[:, k, :],
                                           k == 0, k == DK - 1)
                    if k0 == DK - 2:
                        mm.then_inc(w_used, 1)

                def attention_turn(i, first, last):
                    for t in range(16):
                        if t + 1 < 16:
                            scores(i, t + 1)
                        elif not last:
                            scores(i + 1, 0)
                        if t == 0 and first:
                            pe.wait_ge(co_ready, l + 1)
                        turn_probs(i, t)
                        if t >= 1:
                            tile_out(i, t - 1, first, last)
                        elif not first:
                            tile_out(i - 1, 15)
                        if t == 2 and not first:
                            pair_out(i - 1, bank[5], (0, 1))
                        if t == 10 and last:
                            pair_out(i, bank[5], (0,))
                        gate_steps(i, t)

                scores(0, 0)
                attention_turn(0, True, False)
                with pe.Fori(1, 4) as i:
                    attention_turn(i, False, False)
                attention_turn(4, False, True)
                tile_out(4, 15)
                pair_out(4, bank[0], (1,))

                for n in range(DK):
                    pe.wait_ge(w_ready, NCH * l + C_BR + n + 1)
                    if n >= 2:
                        pe.wait_ge(br_mul, 8 * l + n - 1)
                    each = (lambda k: pe.wait_ge(abc_ready, 8 * l + k + 1)) if n == 0 else None
                    slot, b = (C_BR + n) % RING, 3 * (n % 2)
                    column_tile(slot, bank[b][:], abc_hi, abc_lo, 0, 2, each)
                    column_tile(slot, bank[b + 1][:], abc_hi, abc_lo, 2, 6, each)
                    column_tile(slot, bank[b + 2][:], abc_hi, abc_lo, 6, 8, each).then_inc(w_used, 1)
                for n in range(DK):
                    pe.wait_ge(w_ready, NCH * l + C_OUT + n + 1)
                    if n >= 2:
                        pe.wait_ge(x_ready, 16 * l + 8 + n - 1)
                    each = (lambda k: pe.wait_ge(m_ready, 8 * l + k + 1)) if n == 0 else None
                    column_tile((C_OUT + n) % RING, bank[6 + n % 2][:], mg_hi, mg_lo, each=each).then_inc(w_used, 1)

                pe.wait_ge(h_ready, 16 * l + 17)
                sum_squares(16 * l + 16)
                with pe.Fori(0, FT // 2) as i:
                    for j in range(4):
                        pe.wait_ge(w_ready, NCH * l + 4 * i + (C_GU + j + 1))
                        pe.wait_ge(gu_evac, 44 * l + 4 * i + (j + 1))
                        column_tile((C_GU + j) % RING, bank[j][:], h_hi, h_lo).then_inc(w_used, 1)

                pe.wait_ge(gu_evac, 44 * l + 48)

                def down(slot, hi, lo, first, last):
                    for n in range(DK):
                        mm = split_product(bank[n][:], w_top[:, slot, n * P:n * P + P],
                                           w_rem[:, slot, n * P:n * P + P], hi, lo, first, last)
                        if last and n < DK - 1:
                            mm.then_inc(dn_done, 1)
                    mm.then_inc(w_used, 1)

                def down_static(f):
                    pe.wait_ge(w_ready, NCH * l + C_DN + f + 1)
                    pe.wait_ge(f_ready, FT * l + f + 1)
                    down((C_DN + f) % RING, act_hi[:, f, :], act_lo[:, f, :], f == 0, f == FT - 1)

                down_static(0)
                down_static(1)
                with pe.Fori(0, 4) as i:
                    for j in range(4):
                        pe.wait_ge(w_ready, NCH * l + 4 * i + (C_DN + 2 + j + 1))
                        pe.wait_ge(f_ready, FT * l + 4 * i + (2 + j + 1))
                        down((C_DN + 2 + j) % RING, flat(act_hi[:, ds(4 * i + (2 + j), 1), :]),
                             flat(act_lo[:, ds(4 * i + (2 + j), 1), :]), False, False)
                for f in range(18, FT):
                    down_static(f)
            sum_squares(16 * LAYERS + 8)

        @block.scalar
        def _(act):
            act.sem_inc(at_exp, 2)
            act.sem_inc(at_ca, 1)
            act.wait_ge(const_in, 64)
            act.wait_ge(eps_set, 6)

            def root(count):
                act.wait_ge(ms_done, count)
                nc.scalar.activation(rstd[:], bank[7][:], ACT.Sqrt, bias=epsb[:, 0:1], scale=1.0 / D
                                     ).then_inc(std_done, 1)

            with act.Fori(0, LAYERS) as l:
                act_order = Chain(act, act_chain, l, 16)
                act.wait_ge(small_in, 32 * l + 32)

                def prep(c, i=None):
                    slot = c % RING
                    if i is None:
                        act.wait_ge(raw_in[slot], 16 * (NCH // RING) * l + 16 * (c // RING + 1))
                    else:
                        act.wait_ge(raw_in[slot], 16 * (NCH // RING) * l + 16 * i + 16 * (c // RING + 1))
                    nc.scalar.copy(w_top[:, slot, :], w_raw[:, slot, :]).then_inc(w_split_hi, 1)

                def norm_tile(k, norm):
                    act.wait_ge(x_ready, 16 * l + 8 * norm + k + 1)
                    if k >= 2:
                        act.wait_ge(h_ready, 16 * l + 8 * norm + k)
                    g = vec[:, (V_FN if norm else V_AN) + k:(V_FN if norm else V_AN) + k + 1]
                    act_order.link(nc.scalar.activation(tmp[:, k % 2, :], x[:, k, :], ACT.Identity, scale=g))
                    nc.scalar.copy(h_hi[:, k, :], tmp[:, k % 2, :]).then_inc(xg_done, 1)

                prep(0)
                for k in range(DK):
                    norm_tile(k, 0)
                prep(1)
                nc.scalar.copy(ng_hi[:], sw[:, W_NG:W_NG + DK * NG]).then_inc(ng_w, 1)
                root(2 * l + 2)

                roped_n = 0
                for c in range(18):
                    prep(c + 2)
                    kind, idx = F1[c][1], F1[c][2]
                    t_in, bias = tmp[:, c % 2, :], vec[:, V_B1N + c:V_B1N + c + 1]
                    act.wait_ge(lin_evac, NLIN * l + c + 1)
                    if kind in ("kc", "k", "q"):
                        s = roped_n % 2
                        if roped_n >= 2:
                            act.wait_ge(roped, 11 * l + roped_n - 1)
                        if kind == "q":
                            if idx == 0:
                                act.wait_ge(qb_done, l + 1)
                            nc.scalar.activation(r_in[:, s, :], t_in, ACT.Identity, bias=qb[:, idx:idx + 1],
                                                 scale=QSCALE).then_inc(y_done, 1)
                        else:
                            nc.scalar.activation(r_in[:, s, :], t_in, ACT.Identity, bias=bias).then_inc(y_done, 1)
                        act.wait_ge(y_done, NLIN * l + c + 1)
                        for quarter in range(4):
                            other = 32 * (quarter ^ 1)
                            act.dma_start(r_sw[32 * quarter:32 * quarter + 32, s, :], r_in[other:other + 32, s, :]
                                          ).then_inc(r_swapped[s], 16)
                        roped_n += 1
                    elif kind == "vc":
                        nc.scalar.activation(cmp_src[:, 1, :], t_in, ACT.Identity, bias=bias).then_inc(y_done, 1)
                    elif kind == "v":
                        if idx >= 2:
                            act.wait_ge(vt_done, 4 * l + idx - 1)
                        nc.scalar.activation(vt[:, idx % 2, :], t_in, ACT.Identity, bias=bias).then_inc(y_done, 1)
                    else:
                        if idx == 1:
                            act.wait_ge(d_ready, 2 * l + 1)
                        nc.scalar.activation(pool_u[:, 16:16 + S], t_in, ACT.Identity, bias=bias).then_inc(y_done, 1)
                act.wait_ge(lin_evac, NLIN * l + 19)
                act.wait_ge(gb_done, l + 1)
                nc.scalar.activation(ng_sig[0:NG, :], tmp[0:NG, 0, :], ACT.Tanh, bias=gb[0:NG, 0:1], scale=0.5
                                     ).then_inc(y_done, 1)

                def blocks_hi(kv):
                    act.wait_ge(cb_ready, 2 * l + kv + 1)
                    nc.scalar.copy(cmp_bhi[:, kv], cmp_b[:, kv]).then_inc(cb_hi, 1)

                blocks_hi(0)
                gate_n = 0
                for m, kind in enumerate(MIX):
                    prep(C_MIX + m + 2)
                    if m in (5, 10):
                        kv = m // 10
                        act.wait_ge(gelu_t, 2 * l + kv + 1)
                        nc.scalar.activation(hid[:, 2, :], hid[:, 1, :], ACT.Tanh, scale=GELU_B).then_inc(gelu_a, 1)
                    if kind == "G":
                        act.wait_ge(lin_evac, NLIN * l + 19 + gate_n + 1)
                        nc.scalar.activation(gates[:, gate_n, :], tmp[:, (19 + gate_n) % 2, :], ACT.Tanh,
                                             bias=gb[:, gate_n + 1:gate_n + 2], scale=0.5).then_inc(y_done, 1)
                        gate_n += 1
                    if m == 1:
                        blocks_hi(1)
                    if m == 3:
                        for t in range(2):
                            act.wait_ge(py_done, 2 * l + 2)
                            nc.scalar.activation(a_out[:, t, :], bank[4 + t][:], ACT.Identity,
                                                 scale=vec[:, V_PS + t:V_PS + t + 1]).then_inc(a_ready, 1)
                    if m == 9:
                        act.wait_ge(cs_arg, l + 1)
                        nc.scalar.activation(cmp_p[:], cmp_s[:], ACT.Exp).then_inc(cs_exp, 1)
                for quad in range(2):
                    act.wait_ge(cpt_done, 2 * l + quad + 1)
                    nc.scalar.copy(pcT[:, quad, :], bank[5 - quad][:]).then_inc(cpt_ready, 1)
                act.wait_ge(co_done, l + 1)
                for pair in range(4):
                    ins = nc.scalar.copy(o_cmp[:, pair, :], bank[2 + pair][:])
                ins.then_inc(co_ready, 1)

                def exp_tile(i, t):
                    n = (t % 4 + 1) * P
                    act.wait_ge(at_max, 80 * l + 16 * i + (t + 1))
                    act.wait_ge(at_t, 80 * l + 16 * i + (t + 1))
                    nc.scalar.activation(probs[:, t % 2, 0:n], bank[t % 2][:, 0:n], ACT.Exp,
                                         bias=row_max[:, t % 2:t % 2 + 1],
                                         accum_out=row_sum[:, t // 4 % 4, 0, t % 4:t % 4 + 1]).then_inc(at_exp, 1)

                def turn(i, last):
                    for t in range(16):
                        if t % 2:
                            qt = t % 4
                            act.wait_ge(at_t, 80 * l + 16 * i + (t + 1 + 2))
                            act.wait_ge(at_pv, 80 * l + 16 * i + (t + 1))
                            nc.scalar.copy(pT[:, 1, 0:qt + 1, :],
                                           bank[3][:, 0:(qt + 1) * P].rearrange("p (a b) -> p a b", b=P)
                                           ).then_inc(at_ca, 1)
                        if t + 1 < 16:
                            exp_tile(i, t + 1)
                        elif not last:
                            exp_tile(i + 1, 0)
                        j = t // 4
                        if t % 4 == 1:
                            prep(C_AT + j + 2, i)
                        if t % 4 == 3:
                            act.wait_ge(lin_evac, NLIN * l + RING * i + (19 + MIX_G + j + 1))
                            nc.scalar.activation(flat(gates[:, ds(RING * i + (MIX_G + j), 1), :]),
                                                 tmp[:, (19 + MIX_G + j) % 2, :], ACT.Tanh,
                                                 bias=gb[:, ds(RING * i + (MIX_G + j + 1), 1)], scale=0.5
                                                 ).then_inc(y_done, 1)

                exp_tile(0, 0)
                with act.Fori(0, 4) as i:
                    turn(i, False)
                turn(4, True)

                act.wait_ge(at_o, 6 * l + 7)
                for k in range(DK):
                    src = a_out[:, k, :] if k < 2 else o_all[:, k - 2, :]
                    nc.scalar.copy(abc_hi[:, k, :], src).then_inc(abc_h, 1)
                for n in range(DK):
                    prep(C_BR + n + 2)
                    act.wait_ge(br_sum, 8 * l + n + 1)
                    nc.scalar.activation(mg_hi[:, n, :], br_m[:, n % 2, :], ACT.Copy, scale=0.5).then_inc(br_hi, 1)
                for n in range(DK):
                    prep(C_OUT + n + 2)
                    norm_tile(n, 1)
                act_order.end()
                root(2 * l + 3)

                def ffn_hi(i, s):
                    act.wait_ge(fa_ready, FT * l + 2 * i + (s + 1))
                    nc.scalar.copy(flat(act_hi[:, ds(2 * i + s, 1), :]), f_a[:, s, :]).then_inc(fa_hi, 1)

                with act.Fori(0, FT // 2) as i:
                    for j in range(4):
                        prep(C_GU + j + 2, i)
                        if j % 2 == 0:
                            act.wait_ge(gu_evac, 44 * l + 4 * i + (4 + j + 1))
                            nc.scalar.activation(f_s[:, j // 2, :], f_g[:, j // 2, :], ACT.Silu
                                                 ).then_inc(silu_done, 1)
                        else:
                            ffn_hi(i, j // 2)
                with act.Fori(0, 5) as i:
                    for j in range(4):
                        prep(C_DN + 2 + j, i)

            root(2 * LAYERS + 2)

        @block.vector
        def _(dve):
            dve.sem_inc(x_ready, DK)
            dve.sem_inc(h_ready, 1)
            dve.sem_inc(at_cd, 1)
            dve.sem_inc(at_o, 1)
            dve.sem_inc(at_scale, 2)
            dve.sem_inc(gu_evac, 4)
            nc.vector.memset(epsb[:], EPS).then_inc(eps_set, 1)
            nc.vector.memset(kcmp[:], 0.0).then_inc(eps_set, 1)
            nc.vector.memset(vcmp[:], 0.0).then_inc(eps_set, 1)
            nc.vector.memset(gt[:], 1.0).then_inc(eps_set, 1)
            dve.wait_ge(const_in, 64)
            nc.vector.tensor_copy(k16[:, 0, :], ident).then_inc(eps_set, 1)
            nc.vector.tensor_copy(k16[:, 1, :], tmp[:, 0, 0:P]).then_inc(eps_set, 1)
            dve.wait_ge(eps_set, 6)

            def reciprocal_root(count):
                dve.wait_ge(std_done, count)
                nc.vector.reciprocal(rstd[:], rstd[:]).then_inc(rstd_done, 1)
                dve.wait_ge(rstd_done, count)
                settle(dve)

            with dve.Fori(0, LAYERS) as l:
                order = Chain(dve, dve_chain, l, DVE_LINKS)
                dve.wait_ge(small_in, 32 * l + 32)

                def prep(c, i=None):
                    slot = c % RING
                    dve.wait_ge(w_split_hi, NCH * l + (c + 1) if i is None else NCH * l + 4 * i + (c + 1))
                    nc.vector.tensor_tensor(w_rem[:, slot, :], w_raw[:, slot, :], w_top[:, slot, :], ALU.subtract
                                            ).then_inc(w_ready, 1)

                def norm_tile(k, norm):
                    dve.wait_ge(xg_done, 16 * l + 8 * norm + k + 1)
                    nc.vector.tensor_tensor(h_lo[:, k, :], tmp[:, k % 2, :], h_hi[:, k, :], ALU.subtract
                                            ).then_inc(h_ready, 1)

                prep(0)
                for k in range(DK):
                    norm_tile(k, 0)
                prep(1)
                nc.vector.tensor_scalar(qb[:, 0:6], vec[:, V_B1N + 6:V_B1N + 12], QSCALE, None, ALU.mult
                                        ).then_inc(qb_done, 1)
                nc.vector.tensor_scalar(gb[:, 0:25], vec[:, V_BNG:V_BNG + 25], 0.5, None, ALU.mult
                                        ).then_inc(gb_done, 1)
                dve.wait_ge(ng_w, l + 1)
                nc.vector.tensor_tensor(ng_lo[:], sw[:, W_NG:W_NG + DK * NG], ng_hi[:], ALU.subtract
                                        ).then_inc(ng_split, 1)
                reciprocal_root(2 * l + 1)

                def store_v(n):
                    dve.wait_ge(vt_done, 4 * l + n + 1)
                    nc.vector.tensor_copy(vs[:, :, n, :], bank[4 + n % 2][:].rearrange("p (t f) -> p t f", t=QT)
                                          ).then_inc(v_ready, 1)

                def pool_difference(t):
                    dve.wait_ge(pool_sum, 2 * l + t + 1)
                    for half, total in ((0, pool_b), (1, pool_c)):
                        r = slice(HD * half, HD * half + HD)
                        order.link(nc.vector.tensor_tensor(
                            pool_d[r, t, 0:16], total[r, 16:32], kon[r, K_INV + 16 * t:K_INV + 16 * t + 16], ALU.mult))
                        nc.vector.tensor_tensor(pool_d[r, t, 0:16], pool_d[r, t, 0:16], pool_u[r, 16:32],
                                                ALU.subtract)
                        ins = nc.vector.scalar_tensor_tensor(
                            out=pool_d[r, t, 16:S], in0=total[r, 32:16 + S], scalar=kon[r, K_INVW + t:K_INVW + t + 1],
                            in1=pool_u[r, 32:16 + S], op0=ALU.mult, op1=ALU.subtract)
                    ins.then_inc(d_ready, 1)

                for c in range(18):
                    prep(c + 2)
                    dve.wait_ge(w_used, NCH * l + c + 1 + RING)
                    if c >= 2:
                        dve.wait_ge(y_done, NLIN * l + c - 1)
                    nc.vector.tensor_tensor(tmp[:, c % 2, :], bank[c % 4][:], rstd[:], ALU.mult).then_inc(lin_evac, 1)
                    if c >= 15:
                        store_v(c - 15)
                store_v(3)
                pool_difference(0)
                dve.wait_ge(ng_done, l + 1)
                dve.wait_ge(y_done, NLIN * l + 17)
                nc.vector.tensor_tensor(tmp[0:NG, 0, :], bank[2][0:NG, :], rstd[0:NG, :], ALU.mult
                                        ).then_inc(lin_evac, 1)

                def gate_tile(n, i=None):
                    if i is None:
                        c, b = C_MIX + [m for m, kind in enumerate(MIX) if kind == "G"][n], (19 + n) % 4
                        dve.wait_ge(w_used, NCH * l + c + 1 + RING)
                        dve.wait_ge(y_done, NLIN * l + 19 + n - 1)
                    else:
                        j = n - MIX_G
                        b = 6 + j % 2
                        dve.wait_ge(w_used, NCH * l + RING * i + (C_AT + j + 1 + RING))
                        dve.wait_ge(y_done, NLIN * l + RING * i + (19 + n - 1))
                    nc.vector.tensor_tensor(tmp[:, (19 + n) % 2, :], bank[b][:], rstd[:], ALU.mult
                                            ).then_inc(lin_evac, 1)

                def blocks_rest(kv):
                    dve.wait_ge(cb_hi, 2 * l + kv + 1)
                    nc.vector.tensor_tensor(cmp_blo[:, kv], cmp_b[:, kv], cmp_bhi[:, kv], ALU.subtract
                                            ).then_inc(cb_lo, 1)

                def gelu(kv):
                    c = C_MIX + (4 if kv == 0 else 10)
                    dve.wait_ge(w_used, NCH * l + c + 1 + RING)
                    u, t_, th = hid[:, 0, :], hid[:, 1, :], hid[:, 2, :]
                    for m in range(2):
                        cols = slice(m * 2 * NCMP, (m + 1) * 2 * NCMP)
                        order.link(nc.vector.tensor_scalar(
                            hid[:, 0, cols], bank[7 - kv][:, cols],
                            vec[:, V_CB1 + 2 * kv + m:V_CB1 + 2 * kv + m + 1], None, ALU.add))
                    order.link(nc.vector.tensor_tensor(t_, u, u, ALU.mult))
                    order.link(nc.vector.tensor_scalar(t_, t_, GELU_A, 1.0, ALU.mult, ALU.add))
                    nc.vector.tensor_tensor(t_, t_, u, ALU.mult).then_inc(gelu_t, 1)
                    dve.wait_ge(gelu_a, 2 * l + kv + 1)
                    order.link(nc.vector.scalar_tensor_tensor(out=t_, in0=th, scalar=1.0, in1=u,
                                                              op0=ALU.add, op1=ALU.mult))
                    nc.vector.tensor_scalar(hid[:, 3 + kv, :], t_, 0.5, None, ALU.mult).then_inc(gelu_done, 1)

                s3 = cmp_s[:].rearrange("p q h n -> p (q h) n")
                p3 = cmp_p[:].rearrange("p q h n -> p (q h) n")
                blocks_rest(0)
                pool_difference(1)
                gate_n = 0
                for m, kind in enumerate(MIX):
                    prep(C_MIX + m + 2)
                    if m == 1:
                        blocks_rest(1)
                    if m == 3:
                        dve.wait_ge(ngt_done, l + 1)
                        nc.vector.tensor_scalar(gt[:, :, 0:NG],
                                                bank[6][:, 0:QT * NG].rearrange("p (q g) -> p q g", q=QT), 0.5, 0.5,
                                                ALU.mult, ALU.add).then_inc(gt_ready, 1)
                    if m == 5:
                        gelu(0)
                    if kind == "G":
                        gate_tile(gate_n)
                        gate_n += 1
                    if m == 7:
                        dve.wait_ge(kc_done, l + 1)
                        nc.vector.tensor_scalar(kcmp[:, :, 0:NCMP],
                                                bank[4][:, 0:2 * NCMP].rearrange("p (g n) -> p g n", g=2),
                                                vec[:, V_CB2:V_CB2 + 1], None, ALU.add).then_inc(kc_ready, 1)
                    if m == 9:
                        dve.wait_ge(cs_done, l + 1)
                        for odd in range(2):
                            order.link(nc.vector.tensor_tensor(
                                cmp_s[:, :, odd:8:2, :],
                                bank[5 - odd][:].rearrange("p (q h n) -> p q h n", q=QT, h=4),
                                cm_neg.unsqueeze(2).to_broadcast([P, QT, 4, NC_PAD]), ALU.add))
                        order.link(nc.vector.tensor_reduce(st_c[:, 0, :], s3, AX.X, ALU.max))
                        nc.vector.tensor_tensor(s3, s3, st_c[:, 0, :].unsqueeze(2).to_broadcast([P, 32, NC_PAD]),
                                                ALU.subtract).then_inc(cs_arg, 1)
                    if m == 10:
                        gelu(1)
                        dve.wait_ge(cs_exp, l + 1)
                        for qt in range(QT):
                            mask = cm_one[:, qt:qt + 1, :].to_broadcast([P, 8, NC_PAD])
                            ins = nc.vector.tensor_tensor(cmp_p[:, qt], cmp_p[:, qt], mask, ALU.mult)
                        order.link(ins)
                        order.link(nc.vector.tensor_reduce(st_c[:, 1, :], p3, AX.X, ALU.add))
                        order.link(nc.vector.tensor_scalar(st_c[:, 1, :], st_c[:, 1, :], 1e-30, None, ALU.max))
                        order.link(nc.vector.reciprocal(st_c[:, 2, :], st_c[:, 1, :]))
                        order.link(nc.vector.tensor_tensor(
                            st_c[:, 3, :].rearrange("p (q h) -> p q h", q=QT),
                            st_c[:, 2, :].rearrange("p (q h) -> p q h", q=QT),
                            gt[:, :, 0:NG].rearrange("p q (h b) -> p q h b", b=3)[:, :, :, 0], ALU.mult))
                        nc.vector.tensor_tensor(p3, p3, st_c[:, 3, :].unsqueeze(2).to_broadcast([P, 32, NC_PAD]),
                                                ALU.mult).then_inc(cp_ready, 1)
                dve.wait_ge(vc_done, l + 1)
                for g in range(2):
                    for a in range(4):
                        r = slice(32 * a, 32 * a + NCMP)
                        ins = nc.vector.tensor_tensor(vcmp[r, g, HD * (a % 2):HD * (a % 2) + HD],
                                                      bank[6][r, g * HD:g * HD + HD], vec[r, V_CB2V:V_CB2V + HD],
                                                      ALU.add)
                ins.then_inc(vc_ready, 1)

                def max_tile(i, t):
                    n = (t % 4 + 1) * P
                    dve.wait_ge(at_s, 80 * l + 16 * i + (t + 1))
                    nc.vector.tensor_reduce(row_max[:, t % 2:t % 2 + 1], bank[t % 2][:, 0:n], AX.X, ALU.max, negate=True
                                            ).then_inc(at_max, 1)

                def scale_head(i, h):
                    dve.wait_ge(at_pv, 80 * l + 16 * i + (4 * h + 4 + 2))
                    total, inverse, scale = (row_sum[:, h, k, :] for k in range(3))
                    order.link(nc.vector.reciprocal(inverse, total))
                    col = 24 if isinstance(i, int) and i == 4 else 6 * i + (3 * (h % 2) + 1 + h // 2)
                    gate = gt[:, :, col:col + 1] if isinstance(col, int) else gt[:, :, ds(col, 1)]
                    order.link(nc.vector.tensor_tensor(scale.unsqueeze(2), inverse.unsqueeze(2), gate, ALU.mult))
                    half = HD * (h % 2)
                    nc.vector.tensor_tensor(
                        o_row[:, h // 2, :, half:half + HD],
                        bank[4 + h % 2][:, 0:QT * HD].rearrange("p (q f) -> p q f", q=QT),
                        scale.unsqueeze(2).to_broadcast([P, QT, HD]), ALU.mult).then_inc(at_scale, 1)

                def turn(i, first, last):
                    for t in range(16):
                        if t + 1 < 16:
                            max_tile(i, t + 1)
                        elif not last:
                            max_tile(i + 1, 0)
                        if t % 2 == 0:
                            qt = t % 4
                            dve.wait_ge(at_t, 80 * l + 16 * i + (t + 1 + 2))
                            dve.wait_ge(at_pv, 80 * l + 16 * i + (t + 1))
                            nc.vector.tensor_copy(pT[:, 0, 0:qt + 1, :],
                                                  bank[2][:, 0:(qt + 1) * P].rearrange("p (a b) -> p a b", b=P)
                                                  ).then_inc(at_cd, 1)
                        if t % 4 == 0:
                            if t > 0:
                                scale_head(i, t // 4 - 1)
                            elif not first:
                                scale_head(i - 1, 3)
                        if t == 3 and not first:
                            dve.wait_ge(ot_done, 6 * l + i)
                            if isinstance(i, int):
                                o, o_c = o_all[:, 3, :], o_cmp[:, 3, :]
                            else:
                                o, o_c = flat(o_all[:, ds(i - 1, 1), :]), flat(o_cmp[:, ds(i - 1, 1), :])
                            nc.vector.tensor_tensor(o, bank[5][:], o_c, ALU.add).then_inc(at_o, 1)
                        if t == 11 and last:
                            dve.wait_ge(ot_done, 6 * l + 5)
                            nc.vector.tensor_copy(o_all[:, 4, :], bank[5][:]).then_inc(at_o, 1)
                        if t % 4 == 2:
                            prep(C_AT + t // 4 + 2, i)
                        if t % 4 == 3:
                            gate_tile(MIX_G + t // 4, i)

                max_tile(0, 0)
                turn(0, True, False)
                with dve.Fori(1, 4) as i:
                    order.enter(i, 3, 8, first=1)
                    turn(i, False, False)
                    order.leave()
                turn(4, False, True)
                scale_head(4, 3)
                dve.wait_ge(ot_done, 6 * l + 6)
                nc.vector.tensor_copy(o_all[:, 5, :], bank[0][:]).then_inc(at_o, 1)

                for k in range(DK):
                    src = a_out[:, k, :] if k < 2 else o_all[:, k - 2, :]
                    dve.wait_ge(abc_h, 8 * l + k + 1)
                    nc.vector.tensor_tensor(abc_lo[:, k, :], src, abc_hi[:, k, :], ALU.subtract
                                            ).then_inc(abc_ready, 1)

                def merged_rest(n):
                    dve.wait_ge(br_hi, 8 * l + n + 1)
                    nc.vector.scalar_tensor_tensor(out=mg_lo[:, n, :], in0=br_m[:, n % 2, :], scalar=0.5,
                                                   in1=mg_hi[:, n, :], op0=ALU.mult, op1=ALU.subtract
                                                   ).then_inc(m_ready, 1)

                for n in range(DK):
                    prep(C_BR + n + 2)
                    dve.wait_ge(w_used, NCH * l + C_BR + n + 1 + RING)
                    if n >= 2:
                        dve.wait_ge(br_sum, 8 * l + n - 1)
                    for b in range(3):
                        ins = nc.vector.scalar_tensor_tensor(
                            out=br_t[:, 3 * (n % 2) + b, :], in0=gates[:, 8 * b + n, :], scalar=1.0,
                            in1=bank[3 * (n % 2) + b][:], op0=ALU.add, op1=ALU.mult)
                    ins.then_inc(br_mul, 1)
                    if n >= 1:
                        merged_rest(n - 1)
                merged_rest(DK - 1)
                for n in range(DK):
                    prep(C_OUT + n + 2)
                    dve.wait_ge(w_used, NCH * l + C_OUT + n + 1 + RING)
                    nc.vector.tensor_tensor(x[:, n, :], bank[6 + n % 2][:], x[:, n, :], ALU.add).then_inc(x_ready, 1)
                    if n >= 1:
                        norm_tile(n - 1, 1)
                norm_tile(DK - 1, 1)
                reciprocal_root(2 * l + 2)

                def ffn_rest(i, s):
                    dve.wait_ge(fa_hi, FT * l + 2 * i + (s + 1))
                    nc.vector.tensor_tensor(flat(act_lo[:, ds(2 * i + s, 1), :]), f_a[:, s, :],
                                            flat(act_hi[:, ds(2 * i + s, 1), :]), ALU.subtract).then_inc(f_ready, 1)

                with dve.Fori(0, FT // 2) as i:
                    for j in range(4):
                        prep(C_GU + j + 2, i)
                        dve.wait_ge(w_used, NCH * l + 4 * i + (C_GU + j + 1 + RING))
                        nc.vector.tensor_tensor((f_u if j % 2 else f_g)[:, j // 2, :], bank[j][:], rstd[:], ALU.mult
                                                ).then_inc(gu_evac, 1)
                        if j == 2:
                            ffn_rest(i, 0)
                    ffn_rest(i, 1)
                with dve.Fori(0, 5) as i:
                    for j in range(4):
                        prep(C_DN + 2 + j, i)
                for n in range(DK):
                    if n < DK - 1:
                        dve.wait_ge(dn_done, 7 * l + n + 1)
                    else:
                        dve.wait_ge(w_used, NCH * l + NCH + RING)
                    nc.vector.tensor_tensor(x[:, n, :], bank[n][:], x[:, n, :], ALU.add).then_inc(x_ready, 1)
                order.end()

            reciprocal_root(2 * LAYERS + 1)
            for n in range(DK):
                nc.vector.scalar_tensor_tensor(out=x[:, n, :], in0=x[:, n, :], scalar=fn[:, n:n + 1], in1=rstd[:],
                                               op0=ALU.mult, op1=ALU.mult).then_inc(fin_done, 1)

        @block.gpsimd
        def _(pool):
            pool.wait_ge(const_in, 64)

            def squares(order, readers, xr):
                pool.wait_ge(ms_done, readers)
                settle(pool)
                order.link(nc.gpsimd.memset(ssq[:], 0.0))
                for k in range(DK):
                    pool.wait_ge(x_ready, xr + k + 1)
                    order.link(nc.gpsimd.tensor_tensor(sq[:], x[:, k, :], x[:, k, :], ALU.mult))
                    nc.gpsimd.tensor_tensor(ssq[:], ssq[:], sq[:], ALU.add).then_inc(ssq_ready, 1)
                    pool.wait_ge(ssq_ready, xr + k + 1)
                    settle(pool)

            with pool.Fori(0, LAYERS) as l:
                order = Chain(pool, pool_self, l, POOL_LINKS)
                squares(order, 2 * l + 1, 16 * l)
                pool.wait_ge(small_in, 32 * l + 32)

                def blocks(kv):
                    pool.wait_ge(cx_in, 128 * l + 64 * kv + 64)
                    for b in range(2):
                        src = cmp_x[:, :, 16 * b:16 * b + 16 * NCMP].rearrange("p g (n r) -> p r g n", r=16)[:, 0:16:2]
                        pos = vec[:, V_POS + 16 * kv + 8 * b:V_POS + 16 * kv + 8 * b + 8]
                        ins = nc.gpsimd.tensor_tensor(
                            cmp_b[:, kv, 8 * b:8 * b + 8, :].rearrange("p j (g n) -> p j g n", g=2), src,
                            pos.unsqueeze(2).unsqueeze(3).to_broadcast([P, 8, 2, NCMP]), ALU.add)
                    ins.then_inc(cb_ready, 1)

                rope_n = 0
                for c in range(18):
                    kind, idx = F1[c][1], F1[c][2]
                    if kind in ("kc", "k", "q"):
                        s = rope_n % 2
                        dst = {"kc": cmp_src, "k": ks, "q": qs}[kind][:, idx, :]
                        pool.wait_ge(r_swapped[s], 64 * (6 - s) * l + 64 * (rope_n // 2 + 1))
                        if rope_n:
                            pool.wait_ge(roped, 11 * l + rope_n)
                        nc.gpsimd.tensor_tensor(r_m[:, 0, :], r_in[:, s, :], cos, ALU.mult)
                        order.link(nc.gpsimd.tensor_tensor(r_m[:, 1, :], r_sw[:, s, :], sin, ALU.mult))
                        nc.gpsimd.tensor_tensor(dst, r_m[:, 0, :], r_m[:, 1, :], ALU.add).then_inc(roped, 1)
                        rope_n += 1
                        if rope_n == len(ROPED):
                            blocks(0)
                    elif kind == "u":
                        if idx == 0:
                            for buf in (pool_u, pool_b, pool_c):
                                ins = nc.gpsimd.memset(buf[:, 0:16], 0.0)
                            order.link(ins)
                        pool.wait_ge(y_done, NLIN * l + c + 1)

                        def window(dst, src, shift):
                            return nc.gpsimd.tensor_tensor(dst[:, 16:16 + S], src[:, 16:16 + S],
                                                           src[:, 16 - shift:16 + S - shift], ALU.add)
                        order.link(window(pool_b, pool_u, 1))
                        if idx == 0:
                            window(pool_c, pool_b, 2).then_inc(pool_sum, 1)
                        else:
                            order.link(window(pool_c, pool_b, 2))
                            order.link(window(pool_b, pool_c, 4))
                            window(pool_c, pool_b, 8).then_inc(pool_sum, 1)
                blocks(1)

                for n in range(DK):
                    pool.wait_ge(br_mul, 8 * l + n + 1)
                    if n >= 2:
                        pool.wait_ge(m_ready, 8 * l + n - 1)
                    pool_mul = nc.gpsimd.tensor_tensor(br_m[:, n % 2, :], br_t[:, 3 * (n % 2), :],
                                                       br_t[:, 3 * (n % 2) + 1, :], ALU.add)
                    pool_mul.then_inc(br_part, 1)
                    pool.wait_ge(br_part, 8 * l + n + 1)
                    nc.gpsimd.tensor_tensor(br_m[:, n % 2, :], br_m[:, n % 2, :], br_t[:, 3 * (n % 2) + 2, :],
                                            ALU.add).then_inc(br_sum, 1)
                squares(order, 2 * l + 2, 16 * l + 8)
                with pool.Fori(0, FT // 2) as i:
                    for s in range(2):
                        pool.wait_ge(silu_done, FT * l + 2 * i + (s + 1))
                        pool.wait_ge(gu_evac, 44 * l + 4 * i + (2 * s + 2 + 4))
                        nc.gpsimd.tensor_tensor(f_a[:, s, :], f_s[:, s, :], f_u[:, s, :], ALU.mult
                                                ).then_inc(fa_ready, 1)
                order.end()
            squares(Chain(pool, pool_self, LAYERS, POOL_LINKS), 2 * LAYERS + 1, 16 * LAYERS)


def tiles_by_k(w):
    k = w.shape[0] // P
    return w.reshape(k, P, -1).transpose(1, 0, 2).reshape(P, -1)


def layout(np, a):
    mixed_gates = [C_MIX + m for m, kind in enumerate(MIX) if kind == "G"]
    hidden_chunks = [C_MIX + m for m, kind in enumerate(MIX) if kind != "G"]
    weights = np.empty((LAYERS * NCH, P, CH), np.float32)
    vectors = np.zeros((LAYERS, P, NV), np.float32)
    small = np.zeros((LAYERS, P, NSW), np.float32)
    for l in range(LAYERS):
        w = weights[l * NCH:(l + 1) * NCH]
        w_in, b_in = a["w_in"][l], a["b_in"][l]
        for c, (col, _, _) in enumerate(F1):
            w[C_F1 + c] = tiles_by_k(w_in[:, col:col + P])
            vectors[l, :, V_B1N + c] = b_in[col:col + P]
        for n in range(24):
            col = BG_COL + n * P
            w[mixed_gates[n] if n < MIX_G else C_AT + n - MIX_G] = tiles_by_k(w_in[:, col:col + P])
            vectors[l, :, V_BG + n] = b_in[col:col + P]
        w1 = a["cmp_w1"][l].reshape(2, 4, 4, P, 256).transpose(0, 1, 3, 2, 4)
        w[hidden_chunks] = w1.reshape(8, P, CH)
        branches = np.concatenate([a["w_br_pool"][l], a["w_br_nsa"][l], a["w_br_moba"][l]], axis=0)
        for n in range(DK):
            w[C_BR + n] = tiles_by_k(branches[:, n * P:n * P + P])
            w[C_OUT + n] = tiles_by_k(a["w_out"][l][:, n * P:n * P + P])
        for f in range(FT):
            w[C_GU + 2 * f] = tiles_by_k(a["w_gate"][l][:, f * P:f * P + P])
            w[C_GU + 2 * f + 1] = tiles_by_k(a["w_up"][l][:, f * P:f * P + P])
            w[C_DN + f] = a["w_down"][l][f * P:f * P + P]
        v = vectors[l]
        v[:, V_AN:V_AN + DK] = a["attn_norm"][l].reshape(DK, P).T
        v[0:NG, V_BNG] = b_in[NG_COL:NG_COL + NG]
        v[:, V_PS:V_PS + 2] = a["pool_scale"][l].reshape(2, P).T
        v[:, V_FN:V_FN + DK] = a["ffn_norm"][l].reshape(DK, P).T
        v[:, V_CB1:V_CB1 + 4] = a["cmp_b1"][l].reshape(4, P).T
        v[0:HD, V_CB2] = v[HD:P, V_CB2] = a["cmp_b2"][l][0]
        v[:, V_POS:V_POS + 32] = a["cmp_pos"][l].reshape(2, 16, P).transpose(2, 0, 1).reshape(P, 32)
        v[:, V_CB2V:V_CB2V + HD] = a["cmp_b2"][l][1][None, :]
        s = small[l]
        s[:, W_NG:W_NG + DK * NG] = tiles_by_k(w_in[:, NG_COL:NG_COL + NG])
        w2 = a["cmp_w2"][l].reshape(2, 2, P, HD)
        for m in range(2):
            s[:, W_2K + m * P:W_2K + m * P + HD] = w2[0, m]
            s[:, W_2K + m * P + HD:W_2K + m * P + P] = w2[0, m]
            s[:, W_2V + m * HD:W_2V + m * HD + HD] = w2[1, m]
        for g in range(4):
            r = HD * (g % 2)
            s[r:r + HD, W_PW + (g // 2) * P + r:W_PW + (g // 2) * P + r + HD] = a["pool_w"][l][g]
    return weights, vectors, small


def constants(np):
    k = np.zeros((P, NK), np.float32)
    k[:, K_ID:K_ID + P] = np.eye(P)
    k[:, K_ONE:K_ONE + P] = 1.0
    inv = (np.float32(10000.0) ** (-np.arange(0, HD, 2, dtype=np.float32) / np.float32(HD))).astype(np.float32)
    angle = np.arange(S, dtype=np.float32)[None, :] * inv[:, None]
    c, s = np.cos(angle), np.sin(angle)
    k[:, K_COS:K_COS + S] = np.concatenate([c, c, c, c])
    k[:, K_SIN:K_SIN + S] = np.concatenate([-s, s, -s, s])
    token = np.arange(S).reshape(QT, P).T[:, :, None]
    n = np.arange(NC_PAD)[None, None, :]
    seen = (CMP_STRIDE * n + 31 <= token) & (n < NCMP)
    k[:, K_CM0:K_CM0 + QT * NC_PAD] = np.where(seen, 0.0, NEG).reshape(P, -1)
    k[:, K_CM1:K_CM1 + QT * NC_PAD] = seen.astype(np.float32).reshape(P, -1)
    for g, window in enumerate((2, 4, 8, 16)):
        r, t = slice(HD * (g % 2), HD * (g % 2) + HD), g // 2
        k[r, K_INV + 16 * t:K_INV + 16 * t + 16] = 1.0 / np.minimum(np.arange(16) + 1, window)
        k[r, K_INVW + t] = 1.0 / window
    causal = np.where(np.arange(P)[None, :] > np.arange(P)[:, None], NEG, 0.0).astype(np.float32)
    return k, causal


def kernel(**inputs):
    import numpy as np
    import concourse.bacc as bacc
    from concourse.bass_utils import run_bass_kernel_spmd

    a = {name: np.asarray(value) for name, value in inputs.items()}
    weights, vectors, small = layout(np, a)
    consts, causal = constants(np)
    arrays = {
        "xT": np.ascontiguousarray(a["x"][0].T.reshape(DK, P, S).transpose(1, 0, 2)),
        "weights": weights, "vectors": vectors, "small": small, "consts": consts, "causal": causal,
        "final_norm": np.ascontiguousarray(a["final_norm"].reshape(DK, P).T),
    }
    nc = bacc.Bacc("TRN2", target_bir_lowering=False, num_devices=1)
    args = [nc.dram_tensor(name, v.shape, mybir.dt.from_np(v.dtype), kind="ExternalInput").ap()
            for name, v in arrays.items()]
    out = nc.dram_tensor("out", (P, DK, S), F32, kind="ExternalOutput").ap()
    trunk(nc, *args, out)
    r = run_bass_kernel_spmd(nc, [arrays], core_ids=[0])
    y = r.results[0]["out"]
    return np.ascontiguousarray(y.transpose(1, 0, 2).reshape(D, S).T)[None]
```

```python
from contextlib import ExitStack

import concourse.bass as bass
from concourse import mybir

ALU = mybir.AluOpType
ACT = mybir.ActivationFunctionType
AX = mybir.AxisListType
F32 = mybir.dt.float32
F32R = mybir.dt.float32r
BF16 = mybir.dt.bfloat16
ds = bass.ds

P = 128
D = 1024
S = 512
LAYERS = 2
DK = D // P
QT = S // P
HD = 64
FF = 2816
FT = FF // P
EPS = 1e-6
NEG = -1e30
QSCALE = HD ** -0.5
CMP_STRIDE = 16
NCMP = (S - 32) // CMP_STRIDE + 1
NC_PAD = 32
GELU_A = 0.044715
GELU_B = 0.7978845608028654

CH = 1024
RING = 4
C_F1, C_MIX, C_AT, C_BR, C_OUT, C_GU, C_DN, NCH = 0, 18, 30, 50, 58, 66, 110, 132
MIX = "GkkGkkGvvvvG"
MIX_G = MIX.count("G")
GATE_AHEAD = 4
K_END, V_END = MIX.rindex("k"), MIX.rindex("v")
NLIN = 43
F1 = [(768, "kc", 0), (896, "vc", 0), (1024, "k", 0), (1280, "k", 1), (1816, "k", 2), (1944, "k", 3),
      (256, "q", 0), (384, "q", 1), (512, "q", 2), (640, "q", 3), (1560, "q", 4), (1688, "q", 5),
      (1152, "v", 0), (1408, "v", 1), (2072, "v", 2), (2200, "v", 3), (0, "u", 0), (128, "u", 1)]
ROPED = [c for c, t in enumerate(F1) if t[1] in ("kc", "k", "q")]
VTILES = [c for c, t in enumerate(F1) if t[1] == "v"]
NG_COL, NG, GT_W = 1536, 24, 32
BG_COL = 2328

V_AN, V_B1N, V_BNG, V_BG, V_PS, V_FN, V_CB2, V_POS, V_CB2V, NV = 0, 8, 26, 27, 51, 53, 61, 62, 94, 158
W_NG, W_2K, W_2V, W_PW, NSW = 0, 192, 448, 576, 832
K_ID, K_ONE, K_COS, K_SIN, K_CM0, K_CM1, K_INV, K_INVW, NK = 0, 128, 256, 768, 1280, 1408, 1536, 1568, 1570


POOL_SQ = 6
DVE_LINKS, POOL_LINKS = 58, 30


def trunk(nc, xT, weights, vectors, small, hidden_bias, consts, causal, final_norm, out):
    KB = 1024
    base = 16640

    def place(name, shape, dt, offset):
        return nc.alloc_sbuf_tensor_at(name, shape, dt, offset=base + offset)

    x = place("x", [P, DK, S], F32, 0)
    h_hi = place("h_hi", [P, DK, S], F32R, 16 * KB)
    h_lo = place("h_lo", [P, DK, S], F32R, 32 * KB)
    abc_hi = place("abc_hi", [P, DK, S], F32R, 16 * KB)
    abc_lo = place("abc_lo", [P, DK, S], F32R, 32 * KB)
    w_raw = place("w_raw", [P, RING, CH], F32, 48 * KB)
    w_rem = place("w_rem", [P, RING, CH], F32R, 48 * KB)
    w_top = place("w_top", [P, RING, CH], F32R, 64 * KB)
    act_hi = place("act_hi", [P, FT, S], F32R, 80 * KB)
    act_lo = place("act_lo", [P, FT, S], F32R, 124 * KB)
    gates = place("gates", [P, 24, S], F32, 80 * KB)
    mg_hi = place("mg_hi", [P, DK, S], F32R, 80 * KB)
    mg_lo = place("mg_lo", [P, DK, S], F32R, 96 * KB)
    sq = place("sq", [P, S], F32, 112 * KB)
    sq_a = place("sq_a", [P, 2, S], F32, 114 * KB)
    cmp_src = place("cmp_src", [P, 2, S], F32, 104 * KB)
    cmp_x = place("cmp_x", [P, 2, S], F32, 108 * KB)
    cmp_b = place("cmp_b", [P, 2, 16, 2 * NCMP], F32, 112 * KB)
    cmp_blo = place("cmp_blo", [P, 2, 16, 2 * NCMP], F32R, 112 * KB)
    cmp_bhi = place("cmp_bhi", [P, 2, 16, 2 * NCMP], F32R, 120 * KB)
    qs = place("qs", [P, 6, S], F32, 128 * KB)
    ks = place("ks", [P, 4, S], F32, 140 * KB)
    vs = place("vs", [P, QT, 4, P], F32, 148 * KB)
    o_all = qs
    pcT = place("pcT", [P, 2, S], F32, 112 * KB)
    o_cmp = place("o_cmp", [P, 4, S], F32, 120 * KB)
    probs = place("probs", [P, 2, S], F32, 156 * KB)
    pT = place("pT", [P, 2, QT, P], F32, 160 * KB)
    pool_u = place("pool_u", [P, 16 + S], F32, 156 * KB)
    pool_b = place("pool_b", [P, 16 + S], F32, 156 * KB + 2112)
    pool_c = place("pool_c", [P, 16 + S], F32, 156 * KB + 4224)
    cmp_s = place("cmp_s", [P, QT, 8, NC_PAD], F32, 156 * KB)
    cmp_p = place("cmp_p", [P, QT, 8, NC_PAD], F32, 160 * KB)
    pool_d = place("pool_d", [P, 2, S], F32, 164 * KB)
    a_out = pool_d
    r_in = place("r_in", [P, 2, S], F32, 168 * KB)
    r_sw = place("r_sw", [P, 2, S], F32, 172 * KB)
    r_m = place("r_m", [P, 2, S], F32, 176 * KB)
    vt = place("vt", [P, 2, S], F32, 180 * KB)
    hid = place("hid", [P, 3, 256], F32, 96 * KB)
    hidT = place("hidT", [P, 2, 2 * 2 * NCMP], F32, 99 * KB)
    cb1 = place("cb1", [P, 2, 256], F32, 102 * KB)
    ng_sig = place("ng_sig", [P, S], F32, 100 * KB)
    st_q = place("st_q", [P, 2, S], F32R, 168 * KB)
    st_kh = place("st_kh", [P, 2, S], F32R, 172 * KB)
    st_k = place("st_k", [P, 2, S], F32, 176 * KB)
    st_kl = place("st_kl", [P, 2, S], F32R, 176 * KB)
    st_v = place("st_v", [P, 2, QT, P], F32, 180 * KB)
    q_hi = place("q_hi", [P, S], F32R, 186 * KB)
    br_t = place("br_t", [P, 6, S], F32, 168 * KB)
    br_m = place("br_m", [P, 2, S], F32, 180 * KB)
    f_g = place("f_g", [P, 2, S], F32, 168 * KB)
    f_s = place("f_s", [P, 2, S], F32, 172 * KB)
    f_u = place("f_u", [P, 2, S], F32, 176 * KB)
    f_a = place("f_a", [P, 2, S], F32, 180 * KB)
    rstd = place("rstd", [P, S], F32, 184 * KB)
    ssq = place("ssq", [P, S], F32, 186 * KB)
    tmp = place("tmp", [P, 2, S], F32, 188 * KB)
    kon = place("kon", [P, NK], F32, 192 * KB)
    o_row = place("o_row", [P, 2, QT, P], F32, 192 * KB + 4 * K_COS)
    o = 192 * KB + 4 * 1576
    vec = place("vec", [P, NV], F32, o); o += 4 * 168
    sw = place("sw", [P, NSW], F32, o); o += 4 * NSW
    ng_hi = place("ng_hi", [P, DK * NG], F32R, o); o += 4 * 192
    ng_lo = place("ng_lo", [P, DK * NG], F32R, o); o += 4 * 192
    k16 = place("k16", [P, 2, P], BF16, o); o += 512
    gt = place("gt", [P, QT, GT_W], F32, o); o += 4 * QT * GT_W
    kcmp = place("kcmp", [P, 2, 2 * NC_PAD], F32, o); o += 512
    vcmp = place("vcmp", [P, 2, P], F32, o); o += 1024
    st_c = place("st_c", [P, 4, 32], F32, o); o += 512
    row_max = place("row_max", [P, 2], F32, o); o += 32
    row_sum = place("row_sum", [P, 4, 3, QT], F32, o); o += 192
    qb = place("qb", [P, 8], F32, o); o += 32
    gb = place("gb", [P, 26], F32, o); o += 128
    epsb = place("epsb", [P, 8], F32, o); o += 32
    fn = place("fn", [P, 8], F32, o); o += 32
    o_end = base + o

    ident = kon[:, K_ID:K_ID + P]
    ones = kon[:, K_ONE:K_ONE + P]
    cos = kon[:, K_COS:K_COS + S]
    sin = kon[:, K_SIN:K_SIN + S]
    cm_neg = kon[:, K_CM0:K_CM0 + QT * NC_PAD].rearrange("p (q n) -> p q n", q=QT)
    cm_one = kon[:, K_CM1:K_CM1 + QT * NC_PAD].rearrange("p (q n) -> p q n", q=QT)
    assert o_end <= nc.sbuf_usable_end, o_end - nc.sbuf_usable_end

    with ExitStack() as ctx:
        def sem(name):
            return ctx.enter_context(nc.semaphore(name))

        bank = [ctx.enter_context(nc.psum_tensor(f"bank{b}", [P, S], F32)) for b in range(8)]

        const_in = sem("const_in")
        mask_in = sem("mask_in")
        mask_set = sem("mask_set")
        x_first = sem("x_first")
        x_rest = sem("x_rest")
        bias_in = sem("bias_in")
        ht_done = sem("ht_done")
        ht_ready = sem("ht_ready")
        small_in = sem("small_in")
        sw_in = sem("sw_in")
        raw_in = [sem(f"raw_in{s}") for s in range(RING)]
        w_split_hi = sem("w_split_hi")
        w_ready = sem("w_ready")
        w_used = sem("w_used")
        x_ready = sem("x_ready")
        xg_done = sem("xg_done")
        h_ready = sem("h_ready")
        ssq_ready = sem("ssq_ready")
        sq_act = sem("sq_act")
        sq_sum = sem("sq_sum")
        sq_used = sem("sq_used")
        ms_done = sem("ms_done")
        std_done = sem("std_done")
        rstd_done = sem("rstd_done")
        ng_done = sem("ng_done")
        lin_evac = sem("lin_evac")
        y_done = sem("y_done")
        r_swapped = [sem(f"r_swapped{s}") for s in range(2)]
        roped = sem("roped")
        vt_done = sem("vt_done")
        v_ready = sem("v_ready")
        ng_split = sem("ng_split")
        ng_w = sem("ng_w")
        gb_done = sem("gb_done")
        qb_done = sem("qb_done")
        pool_sum = sem("pool_sum")
        d_ready = sem("d_ready")
        py_done = sem("py_done")
        a_ready = sem("a_ready")
        ngt_done = sem("ngt_done")
        gt_ready = sem("gt_ready")
        cx_in = sem("cx_in")
        cb_ready = sem("cb_ready")
        cb_hi = sem("cb_hi")
        cb_lo = sem("cb_lo")
        gelu_t = sem("gelu_t")
        gelu_a = sem("gelu_a")
        gelu_done = sem("gelu_done")
        kc_done = sem("kc_done")
        kc_ready = sem("kc_ready")
        cs_done = sem("cs_done")
        cs_arg = sem("cs_arg")
        cs_exp = sem("cs_exp")
        cp_ready = sem("cp_ready")
        vc_done = sem("vc_done")
        vc_ready = sem("vc_ready")
        cpt_done = sem("cpt_done")
        cpt_ready = sem("cpt_ready")
        co_done = sem("co_done")
        co_ready = sem("co_ready")
        trig_in = sem("trig_in")
        q_rounded = sem("q_rounded")
        q_split = sem("q_split")
        k_rounded = sem("k_rounded")
        k_ready = sem("k_ready")
        staged_q = [sem(f"staged_q{s}") for s in range(2)]
        staged_k = [sem(f"staged_k{s}") for s in range(2)]
        staged_v = [sem(f"staged_v{s}") for s in range(2)]
        at_s = sem("at_s")
        at_max = sem("at_max")
        at_exp = sem("at_exp")
        at_scale = sem("at_scale")
        at_t = sem("at_t")
        at_ca = sem("at_ca")
        at_cd = sem("at_cd")
        at_pv = sem("at_pv")
        ot_done = sem("ot_done")
        at_o = sem("at_o")
        abc_h = sem("abc_h")
        abc_ready = sem("abc_ready")
        br_mul = sem("br_mul")
        br_sum = sem("br_sum")
        br_hi = sem("br_hi")
        m_ready = sem("m_ready")
        gu_evac = sem("gu_evac")
        silu_done = sem("silu_done")
        fa_ready = sem("fa_ready")
        fa_hi = sem("fa_hi")
        f_ready = sem("f_ready")
        dn_done = sem("dn_done")
        dve_chain = sem("dve_chain")
        pool_self = sem("pool_self")
        br_part = sem("br_part")
        eps_set = sem("eps_set")
        passed = sem("passed")
        fin_done = sem("fin_done")
        stored = sem("stored")


        class Chain:

            def __init__(self, eng, s, l, per_layer):
                self.eng, self.s, self.base, self.k, self.per = eng, s, l * per_layer, 0, per_layer

            def link(self, ins):
                ins.then_inc(self.s, 1)
                self.k += 1
                self.eng.wait_ge(self.s, self.base + self.k)

            def enter(self, i, n, step, first=0):
                self.outer = (self.base, self.k, n, step, first)
                self.base = self.base + i * step
                self.k -= first * step

            def leave(self):
                base, k, n, step, first = self.outer
                assert self.k - k == step - first * step, (self.s, self.k - k)
                self.base, self.k = base, k + n * step

            def end(self):
                assert self.k == self.per, (self.s, self.k)

        def flat_rows(dram, i):
            return dram[ds(i, 1)].rearrange("a p n -> p (a n)")

        def settle(eng):
            eng.sem_inc(passed, 1)

        def flat(ap):
            return ap.rearrange("p a s -> p (a s)")

        block = ctx.enter_context(nc.Block())

        @block.sync
        def _(sp):
            sp.dma_start(x[:, 0:2, :], xT[:, 0:2, :]).then_inc(x_first, 16)
            with sp.Fori(0, LAYERS) as l:
                sp.wait_ge(h_ready, 16 * l + 1)
                sp.dma_start(vec[:], flat_rows(vectors, l)).then_inc(small_in, 16)

                def loads(first, n):
                    with sp.Fori(0, n // RING) as i:
                        for j in range(RING):
                            slot = (first + j) % RING
                            sp.wait_ge(w_used, NCH * l + RING * i + (first + j + 1))
                            sp.dma_start(w_raw[:, slot, :], flat_rows(weights, NCH * l + RING * i + (first + j))
                                         ).then_inc(raw_in[slot], 16)

                def stack_tokens(kv):
                    if kv == 0:
                        sp.wait_ge(roped, 11 * l + 1)
                    else:
                        sp.wait_ge(y_done, NLIN * l + 2)
                        sp.wait_ge(cb_ready, 2 * l + 1)
                    for g in range(2):
                        src = cmp_src[HD * g:HD * g + HD, kv, :]
                        sp.dma_start(cmp_x[0:HD, g, :], src).then_inc(cx_in, 16)
                        sp.dma_start(cmp_x[HD:P, g, 0:S - 1], src[:, 1:S]).then_inc(cx_in, 16)

                def load_one(c, i=None):
                    at_c = NCH * l + c if i is None else NCH * l + RING * i + c
                    sp.wait_ge(w_used, at_c + 1)
                    sp.dma_start(w_raw[:, c % RING, :], flat_rows(weights, at_c)).then_inc(raw_in[c % RING], 16)

                def stage_q(head, q_rest):
                    r = slice(HD * head, HD * head + HD)
                    sp.dma_start(st_q[0:HD, head, :].bitcast(F32), q_hi[r, :].bitcast(F32)).then_inc(staged_q[head], 16)
                    sp.dma_start(st_q[HD:P, head, :].bitcast(F32), q_rest[r, :]).then_inc(staged_q[head], 16)

                def stage_k(s, kv_tile, g):
                    for half in range(2):
                        sp.dma_start(st_k[HD * half:HD * half + HD, s, :], ks[HD * g:HD * g + HD, kv_tile, :]
                                     ).then_inc(staged_k[s], 16)

                def stage_v(s, kv_tile, heads):
                    for half, g in enumerate(heads):
                        sp.dma_start(st_v[:, s, :, HD * half:HD * half + HD],
                                     vs[:, :, kv_tile, HD * g:HD * g + HD]).then_inc(staged_v[s], 16)

                def turn(i, q_src, k_srcs, v_tiles, heads):
                    load_one(C_AT + RING, i)
                    sp.wait_ge(at_s, 80 * l + 16 * i + 8)
                    stage_k(0, *k_srcs[0])
                    load_one(C_AT + RING + 1, i)
                    sp.wait_ge(at_pv, 80 * l + 16 * i + (8 + 2))
                    stage_v(0, v_tiles[0], heads)
                    sp.wait_ge(at_s, 80 * l + 16 * i + 12)
                    settle(sp)
                    sp.wait_ge(q_split, 6 * l + i + 2)
                    stage_q(0, q_src)
                    load_one(C_AT + RING + 2, i)
                    sp.wait_ge(at_s, 80 * l + 16 * i + 16)
                    stage_q(1, q_src)
                    stage_k(1, *k_srcs[1])
                    load_one(C_AT + RING + 3, i)
                    sp.wait_ge(at_pv, 80 * l + 16 * i + (16 + 2))
                    stage_v(1, v_tiles[1], heads)

                loads(0, 4)
                sp.dma_start(sw[:], flat_rows(small, l)).then_inc(sw_in, 16)
                sp.dma_start(kon[:, K_COS:K_CM0], consts[:, K_COS:K_CM0]).then_inc(trig_in, 16)
                loads(4, 12)
                sp.dma_start(flat(cb1[:]), flat_rows(hidden_bias, l)).then_inc(bias_in, 16)
                stack_tokens(0)
                loads(16, 4)
                stack_tokens(1)
                loads(20, 4)
                sp.wait_ge(roped, 11 * l + 11)
                sp.wait_ge(v_ready, 4 * l + 4)
                for s in range(2):
                    stage_k(s, s, 0)
                    stage_v(s, s, (0, 0))
                loads(24, 8)
                load_one(32)
                sp.wait_ge(q_split, 6 * l + 1)
                for head in range(2):
                    stage_q(head, qs[:, 0, :])
                load_one(33)
                for g, turns in ((0, (0, 1)), (1, (1, 3))):
                    with sp.Fori(*turns) as i:
                        turn(i, flat(qs[:, ds(i + 1, 1), :]), ((0, g), (1, g)), (0, 1), (g, g))
                turn(3, qs[:, 4, :], ((2, 0), (2, 1)), (2, 3), (0, 1))
                for head in range(2):
                    sp.wait_ge(at_s, 80 * l + 64 + 4 * head + 4)
                    if head == 0:
                        settle(sp)
                        sp.wait_ge(q_split, 6 * l + 6)
                    stage_q(head, qs[:, 5, :])
                    stage_k(head, 3, head)
                    load_one(C_AT + 5 * RING + head)
                for c in range(C_AT + 5 * RING + 2, 56):
                    load_one(c)
                loads(56, 76)
            for n in range(DK):
                sp.wait_ge(fin_done, n + 1)
                sp.dma_start(out[:, n, :], x[:, n, :]).then_inc(stored, 16)
            sp.wait_ge(stored, 16 * DK)

        @block.tensor
        def _(pe):
            pe.sem_inc(w_used, RING)
            pe.sem_inc(ms_done, 1)
            pe.sem_inc(at_pv, 2)
            pe.sem_inc(at_t, 2)
            pe.wait_ge(eps_set, 4)
            pe.wait_ge(mask_set, 2)

            def split_product(dst, top, rem, hi, lo, first, last, skip=False):
                nc.tensor.matmul(dst, top, hi, start=first, stop=False, skip_group_check=skip)
                nc.tensor.matmul(dst, rem, hi, start=False, stop=False, skip_group_check=skip)
                return nc.tensor.matmul(dst, top, lo, start=False, stop=last, skip_group_check=skip)

            def column_tile(slot, dst, hi, lo, k0=0, k1=DK, each=None):
                for k in range(k0, k1):
                    if each is not None:
                        each(k)
                    mm = split_product(dst, w_top[:, slot, k * P:k * P + P], w_rem[:, slot, k * P:k * P + P],
                                       hi[:, k, :], lo[:, k, :], k == k0, k == k1 - 1)
                return mm

            def sum_squares(norm):
                pe.wait_ge(ssq_ready, POOL_SQ * norm + POOL_SQ)
                nc.tensor.matmul(bank[7][:], ones, ssq[:], start=True, stop=False)
                pe.wait_ge(sq_sum, norm + 1)
                nc.tensor.matmul(bank[7][:], ones, sq_a[:, 0, :], start=False, stop=True).then_inc(ms_done, 1)

            with pe.Fori(0, LAYERS) as l:
                def turn_v(n):
                    pe.wait_ge(y_done, NLIN * l + VTILES[n] + 1)
                    if n >= 2:
                        pe.wait_ge(v_ready, 4 * l + n - 1)
                    for t in range(QT):
                        mm = nc.tensor.transpose(bank[4 + n % 2][:, t * P:t * P + P],
                                                 vt[:, n % 2, t * P:t * P + P], ident)
                    mm.then_inc(vt_done, 1)

                for c in range(18):
                    pe.wait_ge(w_ready, NCH * l + c + 1)
                    if c >= 4:
                        pe.wait_ge(lin_evac, NLIN * l + c - 3)
                    each = (lambda k: pe.wait_ge(h_ready, 16 * l + k + 2)) if c == 0 else None
                    column_tile(c % RING, bank[c % 4][:], h_hi, h_lo, each=each).then_inc(w_used, 1)
                    if c == 2:
                        sum_squares(2 * l)
                    if c - 2 in VTILES:
                        turn_v(VTILES.index(c - 2))
                pe.wait_ge(ng_split, l + 1)
                pe.wait_ge(lin_evac, NLIN * l + 15)
                for k in range(DK):
                    mm = split_product(bank[2][0:NG, :], ng_hi[:, k * NG:k * NG + NG], ng_lo[:, k * NG:k * NG + NG],
                                       h_hi[:, k, :], h_lo[:, k, :], k == 0, k == DK - 1)
                mm.then_inc(ng_done, 1)

                def hidden_chunk(c, kv, q):
                    pe.wait_ge(w_ready, NCH * l + c + 1)
                    for jj in range(4):
                        top, rem = (w[:, c % RING, jj * 256:jj * 256 + 256] for w in (w_top, w_rem))
                        hi, lo = (b[:, kv, 4 * q + jj, :] for b in (cmp_bhi, cmp_blo))
                        dst = bank[7 - kv][0:2 * NCMP, 0:256]
                        nc.tensor.matmul(dst, hi, top, start=q == 0 and jj == 0, stop=False)
                        nc.tensor.matmul(dst, hi, rem, start=False, stop=False)
                        mm = nc.tensor.matmul(dst, lo, top, start=False, stop=q == 3 and jj == 3)
                    mm.then_inc(w_used, 1)

                def turn_hidden(kv):
                    pe.wait_ge(gelu_done, 2 * l + kv + 1)
                    for m in range(2):
                        mm = nc.tensor.matmul(bank[7 - kv][:, 256 + m * 2 * NCMP:256 + (m + 1) * 2 * NCMP],
                                              hid[0:2 * NCMP, 1, m * P:m * P + P], ident[0:2 * NCMP, 0:2 * NCMP],
                                              start=True, stop=True)
                    mm.then_inc(ht_done, 1)

                gate_n, hidden_n = 0, 0
                for m, kind in enumerate(MIX):
                    c = C_MIX + m
                    if kind == "G":
                        pe.wait_ge(w_ready, NCH * l + c + 1)
                        pe.wait_ge(lin_evac, NLIN * l + 19 + gate_n - 3)
                        column_tile(c % RING, bank[(19 + gate_n) % 4][:], h_hi, h_lo).then_inc(w_used, 1)
                        gate_n += 1
                    else:
                        if hidden_n % 4 == 0:
                            pe.wait_ge(cb_lo, 2 * l + hidden_n // 4 + 1)
                            if kind == "v":
                                pe.wait_ge(gt_ready, l + 1)
                        hidden_chunk(c, hidden_n // 4, hidden_n % 4)
                        hidden_n += 1
                    if m == 2:
                        pe.wait_ge(d_ready, 2 * l + 2)
                        pe.wait_ge(v_ready, 4 * l + 4)
                        for t in range(2):
                            nc.tensor.matmul(bank[4 + t][:], sw[:, W_PW + t * P:W_PW + t * P + P], pool_d[:, t, :],
                                             start=True, stop=True).then_inc(py_done, 1)
                        pe.wait_ge(y_done, NLIN * l + 19)
                        settle(pe)
                        for t in range(QT):
                            mm = nc.tensor.transpose(bank[6][:, t * NG:t * NG + NG], ng_sig[0:NG, t * P:t * P + P],
                                                     ident[0:NG, 0:NG])
                        mm.then_inc(ngt_done, 1)
                    if m == K_END + 1:
                        turn_hidden(0)
                        pe.wait_ge(ht_ready, 2 * l + 1)
                        pe.wait_ge(a_ready, 2 * l + 2)
                        for half in range(2):
                            mm = nc.tensor.matmul(bank[4][:, 0:2 * NCMP], sw[:, W_2K + half * P:W_2K + half * P + P],
                                                  hidT[:, 0, half * 2 * NCMP:(half + 1) * 2 * NCMP],
                                                  start=half == 0, stop=half == 1)
                        mm.then_inc(kc_done, 1)
                    if m == K_END + 2:
                        pe.wait_ge(kc_ready, l + 1)
                        pe.wait_ge(roped, 11 * l + 11)
                        for qt in range(QT):
                            for pair in range(4):
                                col = (qt % 2 * 4 + pair) * 2 * NC_PAD
                                mm = nc.tensor.matmul(bank[5 - qt // 2][:, col:col + 2 * NC_PAD],
                                                      qs[:, pair, qt * P:qt * P + P], kcmp[:, pair // 2, :],
                                                      start=True, stop=True)
                        mm.then_inc(cs_done, 1)

                def gate_steps(i, t):
                    j, k0 = t // 4, 2 * (t % 4)
                    c = C_AT + j
                    if k0 == 0:
                        pe.wait_ge(w_ready, NCH * l + RING * i + (c + 1))
                        pe.wait_ge(lin_evac, NLIN * l + RING * i + (19 + MIX_G + j - 1))
                    for k in (k0, k0 + 1):
                        mm = split_product(bank[7 - j % 2][:], w_top[:, c % RING, k * P:k * P + P],
                                           w_rem[:, c % RING, k * P:k * P + P], h_hi[:, k, :], h_lo[:, k, :],
                                           k == 0, k == DK - 1)
                    if k0 == DK - 2:
                        mm.then_inc(w_used, 1)

                for t in range(GATE_AHEAD):
                    gate_steps(0, t)
                turn_hidden(1)
                pe.wait_ge(ht_ready, 2 * l + 2)
                for g in range(2):
                    for a in range(4):
                        for m in range(2):
                            mm = nc.tensor.matmul(bank[6][32 * a:32 * a + NCMP, g * HD:g * HD + HD],
                                                  hidT[:, 1, (m * 2 + g) * NCMP:(m * 2 + g + 1) * NCMP],
                                                  sw[:, W_2V + m * HD:W_2V + m * HD + HD], start=m == 0, stop=m == 1)
                mm.then_inc(vc_done, 1)
                pe.wait_ge(cp_ready, l + 1)
                for quad in range(2):
                    for qt in range(QT):
                        mm = nc.tensor.transpose(
                            bank[5 - quad][:, qt * P:qt * P + P],
                            cmp_p[:, qt, 4 * quad:4 * quad + 4, :].rearrange("p h n -> p (h n)"), ident)
                    mm.then_inc(cpt_done, 1)
                pe.wait_ge(vc_ready, l + 1)
                pe.wait_ge(cpt_ready, 2 * l + 2)
                pe.wait_ge(lin_evac, NLIN * l + 19 + MIX_G)
                for pair in range(4):
                    half = HD * (pair % 2)
                    mm = nc.tensor.matmul(bank[2 + pair][:], vcmp[half:half + HD, pair // 2, :],
                                          pcT[half:half + HD, pair // 2, :], start=True, stop=True)
                mm.then_inc(co_done, 1)


                def scores(i, t, moba=False):
                    h, qt = t // 4, t % 4
                    head, slot = h % 2, h % 2 if moba else h // 2
                    if qt == 0 and (h < 2 or moba):
                        pe.wait_ge(staged_q[head], 192 * l + (32 * i + 32 if h < 2 else 192))
                    if qt == 0 and (h % 2 == 0 or moba):
                        pe.wait_ge(k_ready, 12 * l + (8 + h + 1 if moba else 2 * i + (h // 2 + 1)))
                    pe.wait_ge(at_exp, 80 * l + 16 * i + (t + 1))
                    n = (qt + 1) * P
                    cols = slice(qt * P, qt * P + P)
                    nc.tensor.matmul(bank[t % 2][:, 0:n], st_q[:, head, cols], st_kh[:, slot, 0:n],
                                     start=True, stop=False)
                    nc.tensor.matmul(bank[t % 2][:, 0:n], st_q[0:HD, head, cols], st_kl[0:HD, slot, 0:n],
                                     start=False, stop=False)
                    nc.tensor.matmul(bank[t % 2][:, qt * P:n], k16[:, 0, :], k16[:, 1, :],
                                     start=False, stop=True).then_inc(at_s, 1)

                def turn_probs(i, t):
                    pe.wait_ge(at_exp, 80 * l + 16 * i + (t + 1 + 2))
                    pe.wait_ge(at_ca if t % 2 else at_cd, 40 * l + 8 * i + (t // 2 + 1))
                    for kt in range(t % 4 + 1):
                        mm = nc.tensor.transpose(bank[2 + t % 2][:, kt * P:kt * P + P],
                                                 probs[:, t % 2, kt * P:kt * P + P], ident)
                    mm.then_inc(at_t, 1)

                def tile_out(i, t, first=False, last=False):
                    h, qt = t // 4, t % 4
                    pe.wait_ge(at_ca if t % 2 else at_cd, 40 * l + 8 * i + (t // 2 + 2))
                    if t % 8 == 0:
                        pe.wait_ge(staged_v[t // 8], 160 * l + 32 * i + 32)
                    if qt == 0:
                        pe.wait_ge(at_scale, 20 * l + 4 * i + (h + 1))
                        if h == 1 and not first:
                            pe.wait_ge(at_o, 6 * l + i + 1)
                        if h == 3 and last:
                            pe.wait_ge(at_o, 6 * l + 6)
                    for kt in range(qt + 1):
                        mm = nc.tensor.matmul(bank[4 + h % 2][:, qt * HD:qt * HD + HD], pT[:, t % 2, kt, :],
                                              st_v[:, h // 2, kt, HD * (h % 2):HD * (h % 2) + HD],
                                              start=kt == 0, stop=kt == qt)
                    mm.then_inc(at_pv, 1)

                def pair_out(i, dst, branches):
                    pe.wait_ge(at_scale, 20 * l + 4 * i + (2 * branches[-1] + 2 + 2))
                    pe.wait_ge(at_o, 6 * l + i + 1)
                    for qt in range(QT):
                        for s in branches:
                            mm = nc.tensor.matmul(dst[:, qt * P:qt * P + P], o_row[:, s, qt, :], ident,
                                                  start=s == branches[0], stop=s == branches[-1])
                    mm.then_inc(ot_done, 1)

                def attention_turn(i, first, last):
                    for t in range(16):
                        if t + 1 < 16:
                            scores(i, t + 1, last)
                        elif not last:
                            scores(i + 1, 0)
                        if t == 0 and first:
                            pe.wait_ge(co_ready, l + 1)
                        turn_probs(i, t)
                        if t >= 1:
                            tile_out(i, t - 1, first, last)
                        elif not first:
                            tile_out(i - 1, 15)
                        if t == 2 and not first:
                            pair_out(i - 1, bank[5], (0, 1))
                        if t == 10 and last:
                            pair_out(i, bank[5], (0,))
                        if t >= GATE_AHEAD or not first:
                            gate_steps(i, t)

                scores(0, 0)
                attention_turn(0, True, False)
                with pe.Fori(1, 4) as i:
                    attention_turn(i, False, False)
                attention_turn(4, False, True)
                tile_out(4, 15)

                for n in range(DK):
                    pe.wait_ge(w_ready, NCH * l + C_BR + n + 1)
                    if n >= 2:
                        pe.wait_ge(br_mul, 8 * l + n - 1)
                    each = (lambda k: pe.wait_ge(abc_ready, 8 * l + k + 1)) if n == 0 else None
                    slot, b = (C_BR + n) % RING, 3 * (n % 2)
                    column_tile(slot, bank[b][:], abc_hi, abc_lo, 0, 2, each)
                    if n == 0:
                        pair_out(4, bank[4], (1,))
                    column_tile(slot, bank[b + 1][:], abc_hi, abc_lo, 2, 6, each)
                    column_tile(slot, bank[b + 2][:], abc_hi, abc_lo, 6, 8, each).then_inc(w_used, 1)
                def out_products(n, k0, k1):
                    slot = (C_OUT + n) % RING
                    for k in range(k0, k1):
                        if n == 0:
                            pe.wait_ge(m_ready, 8 * l + k + 1)
                        mm = split_product(bank[6 + n % 2][:], w_top[:, slot, k * P:k * P + P],
                                           w_rem[:, slot, k * P:k * P + P], mg_hi[:, k, :], mg_lo[:, k, :],
                                           k == 0, k == DK - 1)
                    if k1 == DK:
                        mm.then_inc(w_used, 1)

                for n in range(2):
                    pe.wait_ge(w_ready, NCH * l + C_OUT + n + 1)
                    out_products(n, 0, DK - 1)
                for n in range(2):
                    out_products(n, DK - 1, DK)
                for n in range(2, DK):
                    pe.wait_ge(w_ready, NCH * l + C_OUT + n + 1)
                    pe.wait_ge(x_ready, 16 * l + 8 + n - 1)
                    out_products(n, 0, DK)

                def gate_up(i, j, each=None):
                    pe.wait_ge(w_ready, NCH * l + 4 * i + (C_GU + j + 1))
                    pe.wait_ge(gu_evac, 44 * l + 4 * i + (j + 1))
                    column_tile((C_GU + j) % RING, bank[j][:], h_hi, h_lo, each=each).then_inc(w_used, 1)

                for j in range(4):
                    gate_up(0, j, (lambda k: pe.wait_ge(h_ready, 16 * l + 8 + k + 2)) if j == 0 else None)
                    if j == 0:
                        sum_squares(2 * l + 1)
                with pe.Fori(1, FT // 2) as i:
                    for j in range(4):
                        gate_up(i, j)

                pe.wait_ge(gu_evac, 44 * l + 48)

                def down(slot, hi, lo, first, last):
                    for n in range(DK):
                        mm = split_product(bank[n][:], w_top[:, slot, n * P:n * P + P],
                                           w_rem[:, slot, n * P:n * P + P], hi, lo, first, last)
                        if last and n < DK - 1:
                            mm.then_inc(dn_done, 1)
                    mm.then_inc(w_used, 1)

                def down_static(f):
                    pe.wait_ge(w_ready, NCH * l + C_DN + f + 1)
                    pe.wait_ge(f_ready, FT * l + f + 1)
                    down((C_DN + f) % RING, act_hi[:, f, :], act_lo[:, f, :], f == 0, f == FT - 1)

                down_static(0)
                down_static(1)
                with pe.Fori(0, 4) as i:
                    for j in range(4):
                        pe.wait_ge(w_ready, NCH * l + 4 * i + (C_DN + 2 + j + 1))
                        pe.wait_ge(f_ready, FT * l + 4 * i + (2 + j + 1))
                        down((C_DN + 2 + j) % RING, flat(act_hi[:, ds(4 * i + (2 + j), 1), :]),
                             flat(act_lo[:, ds(4 * i + (2 + j), 1), :]), False, False)
                for f in range(18, FT):
                    down_static(f)
            for k in range(DK):
                pe.wait_ge(sq_act, 4 * LAYERS + k + 1)
                ins = nc.tensor.matmul(bank[0][:], ones, sq_a[:, k % 2, :], start=k == 0, stop=k == DK - 1)
                ins.then_inc(ms_done if k == DK - 1 else sq_used, 1)

        @block.scalar
        def _(act):
            act.sem_inc(at_exp, 2)
            act.sem_inc(at_ca, 1)
            act.dma_start(probs[:, 0, 0:P], causal).then_inc(mask_in, 16)
            act.dma_start(kon[:, 0:K_COS], consts[:, 0:K_COS]).then_inc(mask_in, 16)
            act.dma_start(x[:, 2:DK, :], xT[:, 2:DK, :]).then_inc(x_rest, 16)
            act.dma_start(kon[:, K_CM0:NK], consts[:, K_CM0:NK]).then_inc(const_in, 16)
            act.dma_start(fn[:], final_norm).then_inc(const_in, 16)
            act.wait_ge(eps_set, 4)
            act.wait_ge(x_first, 16)

            def root(count, b=7):
                act.wait_ge(ms_done, count)
                nc.scalar.activation(rstd[:], bank[b][:], ACT.Sqrt, bias=epsb[:, 0:1], scale=1.0 / D
                                     ).then_inc(std_done, 1)

            with act.Fori(0, LAYERS) as l:
                act.wait_ge(small_in, 16 * l + 16)

                def prep(c, i=None):
                    slot = c % RING
                    if i is None:
                        act.wait_ge(raw_in[slot], 16 * (NCH // RING) * l + 16 * (c // RING + 1))
                    else:
                        act.wait_ge(raw_in[slot], 16 * (NCH // RING) * l + 16 * i + 16 * (c // RING + 1))
                    nc.scalar.copy(w_top[:, slot, :], w_raw[:, slot, :]).then_inc(w_split_hi, 1)

                def norm_tile(k, norm):
                    act.wait_ge(x_ready, 16 * l + 8 * norm + k + 1)
                    g = vec[:, (V_FN if norm else V_AN) + k:(V_FN if norm else V_AN) + k + 1]
                    nc.scalar.activation(h_hi[:, k, :], x[:, k, :], ACT.Identity, scale=g).then_inc(xg_done, 1)

                def squares(norm):
                    act.wait_ge(ms_done, norm + 1)
                    for k in range(POOL_SQ, DK):
                        act.wait_ge(x_ready, 8 * norm + k + 1)
                        nc.scalar.activation(sq_a[:, k - POOL_SQ, :], x[:, k, :], ACT.Square).then_inc(sq_act, 1)

                prep(0)
                for k in range(DK):
                    if k == 2:
                        act.wait_ge(x_rest, 16)
                    norm_tile(k, 0)
                prep(1)
                squares(2 * l)
                for c in (2, 3, 4):
                    prep(c)
                act.wait_ge(sw_in, 16 * l + 16)
                nc.scalar.copy(ng_hi[:], sw[:, W_NG:W_NG + DK * NG]).then_inc(ng_w, 1)
                root(2 * l + 2)

                def blocks_hi(kv):
                    act.wait_ge(cb_ready, 2 * l + kv + 1)
                    nc.scalar.copy(cmp_bhi[:, kv], cmp_b[:, kv]).then_inc(cb_hi, 1)

                roped_n = 0
                for c in range(18):
                    if 2 <= c < 17:
                        prep(c + 3)
                    kind, idx = F1[c][1], F1[c][2]
                    t_in, bias = tmp[:, c % 2, :], vec[:, V_B1N + c:V_B1N + c + 1]
                    act.wait_ge(lin_evac, NLIN * l + c + 1)
                    if kind in ("kc", "k", "q"):
                        s = roped_n % 2
                        if roped_n >= 2:
                            act.wait_ge(roped, 11 * l + roped_n - 1)
                        if kind == "q":
                            if idx == 0:
                                act.wait_ge(qb_done, l + 1)
                            nc.scalar.activation(r_in[:, s, :], t_in, ACT.Identity, bias=qb[:, idx:idx + 1],
                                                 scale=QSCALE).then_inc(y_done, 1)
                        else:
                            nc.scalar.activation(r_in[:, s, :], t_in, ACT.Identity, bias=bias).then_inc(y_done, 1)
                        act.wait_ge(y_done, NLIN * l + c + 1)
                        for quarter in range(4):
                            other = 32 * (quarter ^ 1)
                            act.dma_start(r_sw[32 * quarter:32 * quarter + 32, s, :], r_in[other:other + 32, s, :]
                                          ).then_inc(r_swapped[s], 16)
                        roped_n += 1
                    elif kind == "vc":
                        nc.scalar.activation(cmp_src[:, 1, :], t_in, ACT.Identity, bias=bias).then_inc(y_done, 1)
                    elif kind == "v":
                        if idx >= 2:
                            act.wait_ge(vt_done, 4 * l + idx - 1)
                        nc.scalar.activation(vt[:, idx % 2, :], t_in, ACT.Identity, bias=bias).then_inc(y_done, 1)
                    else:
                        if idx == 1:
                            act.wait_ge(d_ready, 2 * l + 1)
                        nc.scalar.activation(pool_u[:, 16:16 + S], t_in, ACT.Identity, bias=bias).then_inc(y_done, 1)
                    if c == 16:
                        blocks_hi(0)
                act.wait_ge(lin_evac, NLIN * l + 19)
                act.wait_ge(gb_done, l + 1)
                nc.scalar.activation(ng_sig[0:NG, :], tmp[0:NG, 0, :], ACT.Tanh, bias=gb[0:NG, 0:1], scale=0.5
                                     ).then_inc(y_done, 1)

                def split_q_hi(pair, first=False):
                    if not first:
                        for head in range(2):
                            act.wait_ge(staged_q[head], 192 * l + 32 * pair)
                    src = qs[:, pair, :] if isinstance(pair, int) else flat(qs[:, ds(pair, 1), :])
                    nc.scalar.copy(q_hi[:], src).then_inc(q_rounded, 1)

                def split_k_hi(s, count):
                    act.wait_ge(staged_k[s], 192 * l + count)
                    nc.scalar.copy(st_kh[:, s, :], st_k[:, s, :]).then_inc(k_rounded, 1)

                gate_n = 0
                for m, kind in enumerate(MIX):
                    prep(C_MIX + m + 2)
                    if m in (K_END + 1, V_END + 1):
                        kv = 0 if m == K_END + 1 else 1
                        act.wait_ge(gelu_t, 2 * l + kv + 1)
                        nc.scalar.activation(hid[0:2 * NCMP, 2, :], hid[0:2 * NCMP, 1, :], ACT.Tanh, scale=GELU_B).then_inc(gelu_a, 1)
                    if kind == "G":
                        act.wait_ge(lin_evac, NLIN * l + 19 + gate_n + 1)
                        nc.scalar.activation(gates[:, gate_n, :], tmp[:, (19 + gate_n) % 2, :], ACT.Tanh,
                                             bias=gb[:, gate_n + 1:gate_n + 2], scale=0.5).then_inc(y_done, 1)
                        gate_n += 1
                    if m == 4:
                        blocks_hi(1)
                    if m == 3:
                        for t in range(2):
                            act.wait_ge(py_done, 2 * l + 2)
                            nc.scalar.activation(a_out[:, t, :], bank[4 + t][:], ACT.Identity,
                                                 scale=vec[:, V_PS + t:V_PS + t + 1]).then_inc(a_ready, 1)
                    if m == K_END + 4:
                        act.wait_ge(cs_arg, l + 1)
                        nc.scalar.activation(cmp_p[:], cmp_s[:], ACT.Exp).then_inc(cs_exp, 1)
                        split_q_hi(0, first=True)
                split_k_hi(0, 32)
                for quad in range(2):
                    act.wait_ge(cpt_done, 2 * l + quad + 1)
                    nc.scalar.copy(pcT[:, quad, :], bank[5 - quad][:]).then_inc(cpt_ready, 1)
                act.wait_ge(co_done, l + 1)
                for pair in range(4):
                    ins = nc.scalar.copy(o_cmp[:, pair, :], bank[2 + pair][:])
                ins.then_inc(co_ready, 1)

                def exp_tile(i, t):
                    n = (t % 4 + 1) * P
                    act.wait_ge(at_max, 80 * l + 16 * i + (t + 1))
                    act.wait_ge(at_t, 80 * l + 16 * i + (t + 1))
                    nc.scalar.activation(probs[:, t % 2, 0:n], bank[t % 2][:, 0:n], ACT.Exp,
                                         bias=row_max[:, t % 2:t % 2 + 1],
                                         accum_out=row_sum[:, t // 4 % 4, 0, t % 4:t % 4 + 1]).then_inc(at_exp, 1)

                def turn(i, last):
                    for t in range(16):
                        if t % 2:
                            qt = t % 4
                            act.wait_ge(at_t, 80 * l + 16 * i + (t + 1 + 2))
                            act.wait_ge(at_pv, 80 * l + 16 * i + (t + 1))
                            nc.scalar.copy(pT[:, 1, 0:qt + 1, :],
                                           bank[3][:, 0:(qt + 1) * P].rearrange("p (a b) -> p a b", b=P)
                                           ).then_inc(at_ca, 1)
                        if t + 1 < 16:
                            exp_tile(i, t + 1)
                        elif not last:
                            exp_tile(i + 1, 0)
                        j = t // 4
                        if t == 1:
                            split_k_hi(1, 32 * i + 32)
                        if t == 5 and not last:
                            split_q_hi(i + 1)
                        if t == 11 and not last:
                            split_k_hi(0, 32 * i + 64)
                        if t == 1 and last:
                            split_q_hi(5)
                        if t in (5, 9) and last:
                            split_k_hi(t // 9, 192)
                        if t % 4 == 1:
                            prep(C_AT + j + 2, i)
                        if t % 4 == 3:
                            act.wait_ge(lin_evac, NLIN * l + RING * i + (19 + MIX_G + j + 1))
                            nc.scalar.activation(flat(gates[:, ds(RING * i + (MIX_G + j), 1), :]),
                                                 tmp[:, (19 + MIX_G + j) % 2, :], ACT.Tanh,
                                                 bias=gb[:, ds(RING * i + (MIX_G + j + 1), 1)], scale=0.5
                                                 ).then_inc(y_done, 1)

                exp_tile(0, 0)
                with act.Fori(0, 4) as i:
                    turn(i, False)
                turn(4, True)

                act.wait_ge(w_used, NCH * l + C_BR + RING)
                for k in range(DK):
                    act.wait_ge(at_o, 6 * l + max(k, 5))
                    src = a_out[:, k, :] if k < 2 else o_all[:, k - 2, :]
                    nc.scalar.copy(abc_hi[:, k, :], src).then_inc(abc_h, 1)

                def merged_hi(n):
                    act.wait_ge(br_sum, 8 * l + n + 1)
                    nc.scalar.activation(mg_hi[:, n, :], br_m[:, n % 2, :], ACT.Copy, scale=0.5).then_inc(br_hi, 1)

                for n in range(DK):
                    prep(C_BR + n + 2)
                    if n >= 1:
                        merged_hi(n - 1)
                merged_hi(DK - 1)
                for n in range(DK):
                    prep(C_OUT + n + 2)
                    norm_tile(n, 1)
                squares(2 * l + 1)
                prep(C_GU + 2)
                root(2 * l + 3)

                def ffn_hi(i, s):
                    act.wait_ge(fa_ready, FT * l + 2 * i + (s + 1))
                    nc.scalar.copy(flat(act_hi[:, ds(2 * i + s, 1), :]), f_a[:, s, :]).then_inc(fa_hi, 1)

                with act.Fori(0, FT // 2) as i:
                    for j in range(4):
                        prep(C_GU + j + 3, i)
                        if j % 2 == 0:
                            act.wait_ge(gu_evac, 44 * l + 4 * i + (4 + j + 1))
                            nc.scalar.activation(f_s[:, j // 2, :], f_g[:, j // 2, :], ACT.Silu
                                                 ).then_inc(silu_done, 1)
                        else:
                            ffn_hi(i, j // 2)
                with act.Fori(0, 4) as i:
                    for j in range(4):
                        prep(C_DN + 3 + j, i)
                for f in range(19, FT):
                    prep(C_DN + f)

            for k in range(DK):
                act.wait_ge(x_ready, 16 * LAYERS + k + 1)
                if k >= 2:
                    act.wait_ge(sq_used, k - 1)
                else:
                    act.wait_ge(ms_done, 2 * LAYERS + 1)
                nc.scalar.activation(sq_a[:, k % 2, :], x[:, k, :], ACT.Square).then_inc(sq_act, 1)
            root(2 * LAYERS + 2, 0)

        @block.vector
        def _(dve):
            dve.sem_inc(x_ready, DK)
            dve.sem_inc(h_ready, 1)
            dve.sem_inc(at_cd, 1)
            dve.sem_inc(at_o, 1)
            dve.sem_inc(at_scale, 2)
            dve.sem_inc(gu_evac, 4)
            nc.vector.memset(epsb[:], EPS).then_inc(eps_set, 1)
            nc.vector.memset(kcmp[:], 0.0).then_inc(eps_set, 1)
            nc.vector.memset(vcmp[:], 0.0).then_inc(eps_set, 1)
            nc.vector.memset(gt[:], 1.0).then_inc(eps_set, 1)
            dve.wait_ge(mask_in, 32)
            nc.vector.tensor_copy(k16[:, 0, :], ident).then_inc(mask_set, 1)
            nc.vector.tensor_copy(k16[:, 1, :], probs[:, 0, 0:P]).then_inc(mask_set, 1)
            dve.wait_ge(eps_set, 4)

            def reciprocal_root(count):
                dve.wait_ge(std_done, count)
                nc.vector.reciprocal(rstd[:], rstd[:]).then_inc(rstd_done, 1)
                dve.wait_ge(rstd_done, count)
                settle(dve)

            with dve.Fori(0, LAYERS) as l:
                order = Chain(dve, dve_chain, l, DVE_LINKS)
                dve.wait_ge(small_in, 16 * l + 16)

                def prep(c, i=None):
                    slot = c % RING
                    dve.wait_ge(w_split_hi, NCH * l + (c + 1) if i is None else NCH * l + 4 * i + (c + 1))
                    nc.vector.tensor_tensor(w_rem[:, slot, :], w_raw[:, slot, :], w_top[:, slot, :], ALU.subtract
                                            ).then_inc(w_ready, 1)

                def norm_tile(k, norm):
                    dve.wait_ge(xg_done, 16 * l + 8 * norm + k + 1)
                    g = vec[:, (V_FN if norm else V_AN) + k:(V_FN if norm else V_AN) + k + 1]
                    nc.vector.scalar_tensor_tensor(out=h_lo[:, k, :], in0=x[:, k, :], scalar=g, in1=h_hi[:, k, :],
                                                   op0=ALU.mult, op1=ALU.subtract).then_inc(h_ready, 1)

                def squares(norm):
                    dve.wait_ge(sq_act, 2 * norm + 2)
                    nc.vector.tensor_tensor(sq_a[:, 0, :], sq_a[:, 0, :], sq_a[:, 1, :], ALU.add).then_inc(sq_sum, 1)

                prep(0)
                for k in range(DK):
                    norm_tile(k, 0)
                prep(1)
                squares(2 * l)
                for c in (2, 3, 4):
                    prep(c)
                nc.vector.tensor_scalar(qb[:, 0:6], vec[:, V_B1N + 6:V_B1N + 12], QSCALE, None, ALU.mult
                                        ).then_inc(qb_done, 1)
                nc.vector.tensor_scalar(gb[:, 0:25], vec[:, V_BNG:V_BNG + 25], 0.5, None, ALU.mult
                                        ).then_inc(gb_done, 1)
                dve.wait_ge(ng_w, l + 1)
                nc.vector.tensor_tensor(ng_lo[:], sw[:, W_NG:W_NG + DK * NG], ng_hi[:], ALU.subtract
                                        ).then_inc(ng_split, 1)
                dve.wait_ge(const_in, 32)
                reciprocal_root(2 * l + 1)

                def blocks_rest(kv):
                    dve.wait_ge(cb_hi, 2 * l + kv + 1)
                    nc.vector.tensor_tensor(cmp_blo[:, kv], cmp_b[:, kv], cmp_bhi[:, kv], ALU.subtract
                                            ).then_inc(cb_lo, 1)

                def store_v(n):
                    dve.wait_ge(vt_done, 4 * l + n + 1)
                    nc.vector.tensor_copy(vs[:, :, n, :], bank[4 + n % 2][:].rearrange("p (t f) -> p t f", t=QT)
                                          ).then_inc(v_ready, 1)

                def pool_difference(t):
                    dve.wait_ge(pool_sum, 2 * l + t + 1)
                    for half, total in ((0, pool_b), (1, pool_c)):
                        r = slice(HD * half, HD * half + HD)
                        order.link(nc.vector.tensor_tensor(
                            pool_d[r, t, 0:16], total[r, 16:32], kon[r, K_INV + 16 * t:K_INV + 16 * t + 16], ALU.mult))
                        nc.vector.tensor_tensor(pool_d[r, t, 0:16], pool_d[r, t, 0:16], pool_u[r, 16:32],
                                                ALU.subtract)
                        ins = nc.vector.scalar_tensor_tensor(
                            out=pool_d[r, t, 16:S], in0=total[r, 32:16 + S], scalar=kon[r, K_INVW + t:K_INVW + t + 1],
                            in1=pool_u[r, 32:16 + S], op0=ALU.mult, op1=ALU.subtract)
                    ins.then_inc(d_ready, 1)

                for c in range(18):
                    dve.wait_ge(w_used, NCH * l + c + 1 + RING)
                    if c >= 2:
                        dve.wait_ge(y_done, NLIN * l + c - 1)
                    nc.vector.tensor_tensor(tmp[:, c % 2, :], bank[c % 4][:], rstd[:], ALU.mult).then_inc(lin_evac, 1)
                    if 2 <= c < 17:
                        prep(c + 3)
                    if c >= 15:
                        store_v(c - 15)
                    if c == 17:
                        blocks_rest(0)
                store_v(3)
                pool_difference(0)
                dve.wait_ge(ng_done, l + 1)
                dve.wait_ge(y_done, NLIN * l + 17)
                nc.vector.tensor_tensor(tmp[0:NG, 0, :], bank[2][0:NG, :], rstd[0:NG, :], ALU.mult
                                        ).then_inc(lin_evac, 1)

                def gate_tile(n, i=None):
                    if i is None:
                        c, b = C_MIX + [m for m, kind in enumerate(MIX) if kind == "G"][n], (19 + n) % 4
                        dve.wait_ge(w_used, NCH * l + c + 1 + RING)
                        dve.wait_ge(y_done, NLIN * l + 19 + n - 1)
                    else:
                        j = n - MIX_G
                        b = 7 - j % 2
                        dve.wait_ge(w_used, NCH * l + RING * i + (C_AT + j + 1 + RING))
                        dve.wait_ge(y_done, NLIN * l + RING * i + (19 + n - 1))
                    nc.vector.tensor_tensor(tmp[:, (19 + n) % 2, :], bank[b][:], rstd[:], ALU.mult
                                            ).then_inc(lin_evac, 1)

                def split_q_lo(pair):
                    dve.wait_ge(q_rounded, 6 * l + pair + 1)
                    q = qs[:, pair, :] if isinstance(pair, int) else flat(qs[:, ds(pair, 1), :])
                    nc.vector.tensor_tensor(q.bitcast(F32R), q, q_hi[:], ALU.subtract).then_inc(q_split, 1)

                def split_k_lo(s, count):
                    dve.wait_ge(k_rounded, 12 * l + count)
                    nc.vector.tensor_tensor(st_kl[0:HD, s, :], st_k[0:HD, s, :], st_kh[0:HD, s, :], ALU.subtract
                                            ).then_inc(k_ready, 1)

                def gelu(kv):
                    c = C_MIX + (V_END if kv else K_END)
                    dve.wait_ge(w_used, NCH * l + c + 1 + RING)
                    dve.wait_ge(bias_in, 16 * l + 16)
                    u, t_, th = (hid[0:2 * NCMP, b, :] for b in range(3))
                    order.link(nc.vector.tensor_tensor(u, bank[7 - kv][0:2 * NCMP, 0:256], cb1[0:2 * NCMP, kv, :],
                                                       ALU.add))
                    order.link(nc.vector.tensor_tensor(t_, u, u, ALU.mult))
                    order.link(nc.vector.tensor_scalar(t_, t_, GELU_A, 1.0, ALU.mult, ALU.add))
                    nc.vector.tensor_tensor(t_, t_, u, ALU.mult).then_inc(gelu_t, 1)
                    dve.wait_ge(gelu_a, 2 * l + kv + 1)
                    nc.vector.scalar_tensor_tensor(out=t_, in0=th, scalar=1.0, in1=u, op0=ALU.add, op1=ALU.mult
                                                   ).then_inc(gelu_done, 1)

                def store_hidden(kv):
                    dve.wait_ge(ht_done, 2 * l + kv + 1)
                    nc.vector.tensor_scalar(hidT[:, kv, :], bank[7 - kv][:, 256:256 + 4 * NCMP], 0.5, None, ALU.mult
                                            ).then_inc(ht_ready, 1)

                s3 = cmp_s[:].rearrange("p q h n -> p (q h) n")
                p3 = cmp_p[:].rearrange("p q h n -> p (q h) n")
                pool_difference(1)
                gate_n = 0
                for m, kind in enumerate(MIX):
                    prep(C_MIX + m + 2)
                    if m == 4:
                        blocks_rest(1)
                    if m == 3:
                        dve.wait_ge(ngt_done, l + 1)
                        nc.vector.tensor_scalar(gt[:, :, 0:NG],
                                                bank[6][:, 0:QT * NG].rearrange("p (q g) -> p q g", q=QT), 0.5, 0.5,
                                                ALU.mult, ALU.add).then_inc(gt_ready, 1)
                    if m == K_END + 1:
                        gelu(0)
                    if kind == "G":
                        gate_tile(gate_n)
                        gate_n += 1
                    if m == K_END + 1:
                        store_hidden(0)
                        dve.wait_ge(kc_done, l + 1)
                        for half in range(2):
                            r = slice(HD * half, HD * half + HD)
                            ins = nc.vector.tensor_scalar(kcmp[r, :, NC_PAD * half:NC_PAD * half + NCMP],
                                                          bank[4][r, 0:2 * NCMP].rearrange("p (g n) -> p g n", g=2),
                                                          vec[r, V_CB2:V_CB2 + 1], None, ALU.add)
                        ins.then_inc(kc_ready, 1)
                    if m == K_END + 3:
                        dve.wait_ge(cs_done, l + 1)
                        for half in range(2):
                            q2 = slice(2 * half, 2 * half + 2)
                            order.link(nc.vector.tensor_tensor(
                                cmp_s[:, q2], bank[5 - half][:].rearrange("p (q h n) -> p q h n", q=2, h=8),
                                cm_neg[:, q2].unsqueeze(2).to_broadcast([P, 2, 8, NC_PAD]), ALU.add))
                        order.link(nc.vector.tensor_reduce(st_c[:, 0, :], s3, AX.X, ALU.max))
                        nc.vector.tensor_tensor(s3, s3, st_c[:, 0, :].unsqueeze(2).to_broadcast([P, 32, NC_PAD]),
                                                ALU.subtract).then_inc(cs_arg, 1)
                    if m == V_END:
                        dve.wait_ge(cs_exp, l + 1)
                        for qt in range(QT):
                            mask = cm_one[:, qt:qt + 1, :].to_broadcast([P, 8, NC_PAD])
                            ins = nc.vector.tensor_tensor(cmp_p[:, qt], cmp_p[:, qt], mask, ALU.mult)
                        order.link(ins)
                        order.link(nc.vector.tensor_reduce(st_c[:, 1, :], p3, AX.X, ALU.add))
                        order.link(nc.vector.tensor_scalar(st_c[:, 1, :], st_c[:, 1, :], 1e-30, None, ALU.max))
                        order.link(nc.vector.reciprocal(st_c[:, 2, :], st_c[:, 1, :]))
                        order.link(nc.vector.tensor_tensor(
                            st_c[:, 3, :].rearrange("p (q h) -> p q h", q=QT),
                            st_c[:, 2, :].rearrange("p (q h) -> p q h", q=QT),
                            gt[:, :, 0:NG].rearrange("p q (h b) -> p q h b", b=3)[:, :, :, 0], ALU.mult))
                        nc.vector.tensor_tensor(p3, p3, st_c[:, 3, :].unsqueeze(2).to_broadcast([P, 32, NC_PAD]),
                                                ALU.mult).then_inc(cp_ready, 1)
                        gelu(1)
                        split_q_lo(0)
                store_hidden(1)
                dve.wait_ge(vc_done, l + 1)
                for g in range(2):
                    for a in range(4):
                        r = slice(32 * a, 32 * a + NCMP)
                        ins = nc.vector.tensor_tensor(vcmp[r, g, HD * (a % 2):HD * (a % 2) + HD],
                                                      bank[6][r, g * HD:g * HD + HD], vec[r, V_CB2V:V_CB2V + HD],
                                                      ALU.add)
                ins.then_inc(vc_ready, 1)
                split_k_lo(0, 1)

                def max_tile(i, t):
                    n = (t % 4 + 1) * P
                    dve.wait_ge(at_s, 80 * l + 16 * i + (t + 1))
                    nc.vector.tensor_reduce(row_max[:, t % 2:t % 2 + 1], bank[t % 2][:, 0:n], AX.X, ALU.max, negate=True
                                            ).then_inc(at_max, 1)

                def scale_head(i, h):
                    dve.wait_ge(at_pv, 80 * l + 16 * i + (4 * h + 4 + 2))
                    total, inverse, scale = (row_sum[:, h, k, :] for k in range(3))
                    order.link(nc.vector.reciprocal(inverse, total))
                    col = 24 if isinstance(i, int) and i == 4 else 6 * i + (3 * (h % 2) + 1 + h // 2)
                    gate = gt[:, :, col:col + 1] if isinstance(col, int) else gt[:, :, ds(col, 1)]
                    order.link(nc.vector.tensor_tensor(scale.unsqueeze(2), inverse.unsqueeze(2), gate, ALU.mult))
                    half = HD * (h % 2)
                    nc.vector.tensor_tensor(
                        o_row[:, h // 2, :, half:half + HD],
                        bank[4 + h % 2][:, 0:QT * HD].rearrange("p (q f) -> p q f", q=QT),
                        scale.unsqueeze(2).to_broadcast([P, QT, HD]), ALU.mult).then_inc(at_scale, 1)

                def turn(i, first, last):
                    for t in range(16):
                        if t + 1 < 16:
                            max_tile(i, t + 1)
                        elif not last:
                            max_tile(i + 1, 0)
                        if t % 2 == 0:
                            qt = t % 4
                            dve.wait_ge(at_t, 80 * l + 16 * i + (t + 1 + 2))
                            dve.wait_ge(at_pv, 80 * l + 16 * i + (t + 1))
                            nc.vector.tensor_copy(pT[:, 0, 0:qt + 1, :],
                                                  bank[2][:, 0:(qt + 1) * P].rearrange("p (a b) -> p a b", b=P)
                                                  ).then_inc(at_cd, 1)
                        if t % 4 == 0:
                            if t > 0:
                                scale_head(i, t // 4 - 1)
                            elif not first:
                                scale_head(i - 1, 3)
                        if t == 3 and not first:
                            dve.wait_ge(ot_done, 6 * l + i)
                            if isinstance(i, int):
                                o, o_c = o_all[:, 3, :], o_cmp[:, 3, :]
                            else:
                                o, o_c = flat(o_all[:, ds(i - 1, 1), :]), flat(o_cmp[:, ds(i - 1, 1), :])
                            nc.vector.tensor_tensor(o, bank[5][:], o_c, ALU.add).then_inc(at_o, 1)
                        if t == 11 and last:
                            dve.wait_ge(ot_done, 6 * l + 5)
                            nc.vector.tensor_copy(o_all[:, 4, :], bank[5][:]).then_inc(at_o, 1)
                        if t == 1:
                            split_k_lo(1, 2 * i + 2)
                        if t == 5 and not last:
                            split_q_lo(i + 1)
                        if t == 11 and not last:
                            split_k_lo(0, 2 * i + 3)
                        if t == 1 and last:
                            split_q_lo(5)
                        if t in (5, 9) and last:
                            split_k_lo(t // 9, 11 + t // 9)
                        if t % 4 == 2:
                            prep(C_AT + t // 4 + 2, i)
                        if t % 4 == 3:
                            gate_tile(MIX_G + t // 4, i)

                max_tile(0, 0)
                turn(0, True, False)
                with dve.Fori(1, 4) as i:
                    order.enter(i, 3, 8, first=1)
                    turn(i, False, False)
                    order.leave()
                turn(4, False, True)
                scale_head(4, 3)
                for k in range(DK):
                    if k == 4:
                        dve.wait_ge(ot_done, 6 * l + 6)
                        nc.vector.tensor_copy(o_all[:, 5, :], bank[4][:]).then_inc(at_o, 1)
                    src = a_out[:, k, :] if k < 2 else o_all[:, k - 2, :]
                    dve.wait_ge(abc_h, 8 * l + k + 1)
                    nc.vector.tensor_tensor(abc_lo[:, k, :], src, abc_hi[:, k, :], ALU.subtract
                                            ).then_inc(abc_ready, 1)

                def merged_rest(n):
                    dve.wait_ge(br_hi, 8 * l + n + 1)
                    nc.vector.scalar_tensor_tensor(out=mg_lo[:, n, :], in0=br_m[:, n % 2, :], scalar=0.5,
                                                   in1=mg_hi[:, n, :], op0=ALU.mult, op1=ALU.subtract
                                                   ).then_inc(m_ready, 1)

                for n in range(DK):
                    prep(C_BR + n + 2)
                    dve.wait_ge(w_used, NCH * l + C_BR + n + 1 + RING)
                    if n >= 2:
                        dve.wait_ge(br_sum, 8 * l + n - 1)
                    for b in range(3):
                        ins = nc.vector.scalar_tensor_tensor(
                            out=br_t[:, 3 * (n % 2) + b, :], in0=gates[:, 8 * b + n, :], scalar=1.0,
                            in1=bank[3 * (n % 2) + b][:], op0=ALU.add, op1=ALU.mult)
                    ins.then_inc(br_mul, 1)
                    if n >= 1:
                        merged_rest(n - 1)
                merged_rest(DK - 1)
                for n in range(DK):
                    prep(C_OUT + n + 2)
                    dve.wait_ge(w_used, NCH * l + C_OUT + n + 1 + RING)
                    nc.vector.tensor_tensor(x[:, n, :], bank[6 + n % 2][:], x[:, n, :], ALU.add).then_inc(x_ready, 1)
                    if n >= 1:
                        norm_tile(n - 1, 1)
                norm_tile(DK - 1, 1)
                squares(2 * l + 1)
                prep(C_GU + 2)
                reciprocal_root(2 * l + 2)

                def ffn_rest(i, s):
                    dve.wait_ge(fa_hi, FT * l + 2 * i + (s + 1))
                    nc.vector.tensor_tensor(flat(act_lo[:, ds(2 * i + s, 1), :]), f_a[:, s, :],
                                            flat(act_hi[:, ds(2 * i + s, 1), :]), ALU.subtract).then_inc(f_ready, 1)

                with dve.Fori(0, FT // 2) as i:
                    for j in range(4):
                        dve.wait_ge(w_used, NCH * l + 4 * i + (C_GU + j + 1 + RING))
                        nc.vector.tensor_tensor((f_u if j % 2 else f_g)[:, j // 2, :], bank[j][:], rstd[:], ALU.mult
                                                ).then_inc(gu_evac, 1)
                        prep(C_GU + j + 3, i)
                        if j == 2:
                            ffn_rest(i, 0)
                    ffn_rest(i, 1)
                with dve.Fori(0, 4) as i:
                    for j in range(4):
                        prep(C_DN + 3 + j, i)
                for f in range(19, FT):
                    prep(C_DN + f)
                for n in range(DK):
                    if n < DK - 1:
                        dve.wait_ge(dn_done, 7 * l + n + 1)
                    else:
                        dve.wait_ge(w_used, NCH * l + NCH + RING)
                    nc.vector.tensor_tensor(x[:, n, :], bank[n][:], x[:, n, :], ALU.add).then_inc(x_ready, 1)
                order.end()

            reciprocal_root(2 * LAYERS + 1)
            for n in range(DK):
                nc.vector.scalar_tensor_tensor(out=x[:, n, :], in0=x[:, n, :], scalar=fn[:, n:n + 1], in1=rstd[:],
                                               op0=ALU.mult, op1=ALU.mult).then_inc(fin_done, 1)

        @block.gpsimd
        def _(pool):
            pool.wait_ge(x_first, 16)

            def squares(order, norm):
                pool.wait_ge(ms_done, norm + 1)
                settle(pool)
                order.link(nc.gpsimd.memset(ssq[:], 0.0))
                for k in range(POOL_SQ):
                    if k == 2:
                        pool.wait_ge(x_rest, 16)
                    pool.wait_ge(x_ready, 8 * norm + k + 1)
                    order.link(nc.gpsimd.tensor_tensor(sq[:], x[:, k, :], x[:, k, :], ALU.mult))
                    nc.gpsimd.tensor_tensor(ssq[:], ssq[:], sq[:], ALU.add).then_inc(ssq_ready, 1)
                    pool.wait_ge(ssq_ready, POOL_SQ * norm + k + 1)
                    settle(pool)

            with pool.Fori(0, LAYERS) as l:
                order = Chain(pool, pool_self, l, POOL_LINKS)
                squares(order, 2 * l)
                pool.wait_ge(small_in, 16 * l + 16)

                def blocks(kv):
                    pool.wait_ge(cx_in, 128 * l + 64 * kv + 64)
                    for b in range(2):
                        src = cmp_x[:, :, 16 * b:16 * b + 16 * NCMP].rearrange("p g (n r) -> p r g n", r=16)[:, 0:16:2]
                        pos = vec[:, V_POS + 16 * kv + 8 * b:V_POS + 16 * kv + 8 * b + 8]
                        ins = nc.gpsimd.tensor_tensor(
                            cmp_b[:, kv, 8 * b:8 * b + 8, :].rearrange("p j (g n) -> p j g n", g=2), src,
                            pos.unsqueeze(2).unsqueeze(3).to_broadcast([P, 8, 2, NCMP]), ALU.add)
                    ins.then_inc(cb_ready, 1)

                pool.wait_ge(trig_in, 16 * l + 16)
                rope_n = 0
                for c in range(18):
                    kind, idx = F1[c][1], F1[c][2]
                    if kind in ("kc", "k", "q"):
                        s = rope_n % 2
                        dst = {"kc": cmp_src, "k": ks, "q": qs}[kind][:, idx, :]
                        pool.wait_ge(r_swapped[s], 64 * (6 - s) * l + 64 * (rope_n // 2 + 1))
                        if rope_n:
                            pool.wait_ge(roped, 11 * l + rope_n)
                        nc.gpsimd.tensor_tensor(r_m[:, 0, :], r_in[:, s, :], cos, ALU.mult)
                        order.link(nc.gpsimd.tensor_tensor(r_m[:, 1, :], r_sw[:, s, :], sin, ALU.mult))
                        nc.gpsimd.tensor_tensor(dst, r_m[:, 0, :], r_m[:, 1, :], ALU.add).then_inc(roped, 1)
                        rope_n += 1
                        if rope_n == len(ROPED):
                            blocks(0)
                    elif kind == "u":
                        if idx == 0:
                            for buf in (pool_u, pool_b, pool_c):
                                ins = nc.gpsimd.memset(buf[:, 0:16], 0.0)
                            order.link(ins)
                        pool.wait_ge(y_done, NLIN * l + c + 1)

                        def window(dst, src, shift):
                            return nc.gpsimd.tensor_tensor(dst[:, 16:16 + S], src[:, 16:16 + S],
                                                           src[:, 16 - shift:16 + S - shift], ALU.add)
                        order.link(window(pool_b, pool_u, 1))
                        if idx == 0:
                            window(pool_c, pool_b, 2).then_inc(pool_sum, 1)
                        else:
                            order.link(window(pool_c, pool_b, 2))
                            order.link(window(pool_b, pool_c, 4))
                            window(pool_c, pool_b, 8).then_inc(pool_sum, 1)
                blocks(1)

                for n in range(DK):
                    pool.wait_ge(br_mul, 8 * l + n + 1)
                    if n >= 2:
                        pool.wait_ge(m_ready, 8 * l + n - 1)
                    pool_mul = nc.gpsimd.tensor_tensor(br_m[:, n % 2, :], br_t[:, 3 * (n % 2), :],
                                                       br_t[:, 3 * (n % 2) + 1, :], ALU.add)
                    pool_mul.then_inc(br_part, 1)
                    pool.wait_ge(br_part, 8 * l + n + 1)
                    nc.gpsimd.tensor_tensor(br_m[:, n % 2, :], br_m[:, n % 2, :], br_t[:, 3 * (n % 2) + 2, :],
                                            ALU.add).then_inc(br_sum, 1)
                squares(order, 2 * l + 1)
                with pool.Fori(0, FT // 2) as i:
                    for s in range(2):
                        pool.wait_ge(silu_done, FT * l + 2 * i + (s + 1))
                        pool.wait_ge(gu_evac, 44 * l + 4 * i + (2 * s + 2 + 4))
                        nc.gpsimd.tensor_tensor(f_a[:, s, :], f_s[:, s, :], f_u[:, s, :], ALU.mult
                                                ).then_inc(fa_ready, 1)
                order.end()


def tiles_by_k(w):
    k = w.shape[0] // P
    return w.reshape(k, P, -1).transpose(1, 0, 2).reshape(P, -1)


def layout(np, a):
    mixed_gates = [C_MIX + m for m, kind in enumerate(MIX) if kind == "G"]
    hidden_chunks = [C_MIX + m for m, kind in enumerate(MIX) if kind != "G"]
    weights = np.empty((LAYERS * NCH, P, CH), np.float32)
    vectors = np.zeros((LAYERS, P, NV), np.float32)
    small = np.zeros((LAYERS, P, NSW), np.float32)
    hidden_bias = np.zeros((LAYERS, P, 512), np.float32)
    for l in range(LAYERS):
        w = weights[l * NCH:(l + 1) * NCH]
        w_in, b_in = a["w_in"][l], a["b_in"][l]
        for c, (col, _, _) in enumerate(F1):
            w[C_F1 + c] = tiles_by_k(w_in[:, col:col + P])
            vectors[l, :, V_B1N + c] = b_in[col:col + P]
        for n in range(24):
            col = BG_COL + n * P
            w[mixed_gates[n] if n < MIX_G else C_AT + n - MIX_G] = tiles_by_k(w_in[:, col:col + P])
            vectors[l, :, V_BG + n] = b_in[col:col + P]
        w1 = a["cmp_w1"][l].reshape(2, 4, 4, P, 256).transpose(0, 1, 3, 2, 4)
        w[hidden_chunks] = w1.reshape(8, P, CH)
        branches = np.concatenate([a["w_br_pool"][l], a["w_br_nsa"][l], a["w_br_moba"][l]], axis=0)
        for n in range(DK):
            w[C_BR + n] = tiles_by_k(branches[:, n * P:n * P + P])
            w[C_OUT + n] = tiles_by_k(a["w_out"][l][:, n * P:n * P + P])
        for f in range(FT):
            w[C_GU + 2 * f] = tiles_by_k(a["w_gate"][l][:, f * P:f * P + P])
            w[C_GU + 2 * f + 1] = tiles_by_k(a["w_up"][l][:, f * P:f * P + P])
            w[C_DN + f] = a["w_down"][l][f * P:f * P + P]
        v = vectors[l]
        v[:, V_AN:V_AN + DK] = a["attn_norm"][l].reshape(DK, P).T
        v[0:NG, V_BNG] = b_in[NG_COL:NG_COL + NG]
        v[:, V_PS:V_PS + 2] = a["pool_scale"][l].reshape(2, P).T
        v[:, V_FN:V_FN + DK] = a["ffn_norm"][l].reshape(DK, P).T
        hidden_bias[l] = a["cmp_b1"][l].reshape(1, 512)
        v[0:HD, V_CB2] = v[HD:P, V_CB2] = a["cmp_b2"][l][0]
        v[:, V_POS:V_POS + 32] = a["cmp_pos"][l].reshape(2, 16, P).transpose(2, 0, 1).reshape(P, 32)
        v[:, V_CB2V:V_CB2V + HD] = a["cmp_b2"][l][1][None, :]
        s = small[l]
        s[:, W_NG:W_NG + DK * NG] = tiles_by_k(w_in[:, NG_COL:NG_COL + NG])
        w2 = a["cmp_w2"][l].reshape(2, 2, P, HD)
        for m in range(2):
            s[:, W_2K + m * P:W_2K + m * P + HD] = w2[0, m]
            s[:, W_2K + m * P + HD:W_2K + m * P + P] = w2[0, m]
            s[:, W_2V + m * HD:W_2V + m * HD + HD] = w2[1, m]
        for g in range(4):
            r = HD * (g % 2)
            s[r:r + HD, W_PW + (g // 2) * P + r:W_PW + (g // 2) * P + r + HD] = a["pool_w"][l][g]
    return weights, vectors, small, hidden_bias


def constants(np):
    k = np.zeros((P, NK), np.float32)
    k[:, K_ID:K_ID + P] = np.eye(P)
    k[:, K_ONE:K_ONE + P] = 1.0
    inv = (np.float32(10000.0) ** (-np.arange(0, HD, 2, dtype=np.float32) / np.float32(HD))).astype(np.float32)
    angle = np.arange(S, dtype=np.float32)[None, :] * inv[:, None]
    c, s = np.cos(angle), np.sin(angle)
    k[:, K_COS:K_COS + S] = np.concatenate([c, c, c, c])
    k[:, K_SIN:K_SIN + S] = np.concatenate([-s, s, -s, s])
    token = np.arange(S).reshape(QT, P).T[:, :, None]
    n = np.arange(NC_PAD)[None, None, :]
    seen = (CMP_STRIDE * n + 31 <= token) & (n < NCMP)
    k[:, K_CM0:K_CM0 + QT * NC_PAD] = np.where(seen, 0.0, NEG).reshape(P, -1)
    k[:, K_CM1:K_CM1 + QT * NC_PAD] = seen.astype(np.float32).reshape(P, -1)
    for g, window in enumerate((2, 4, 8, 16)):
        r, t = slice(HD * (g % 2), HD * (g % 2) + HD), g // 2
        k[r, K_INV + 16 * t:K_INV + 16 * t + 16] = 1.0 / np.minimum(np.arange(16) + 1, window)
        k[r, K_INVW + t] = 1.0 / window
    causal = np.where(np.arange(P)[None, :] > np.arange(P)[:, None], NEG, 0.0).astype(np.float32)
    return k, causal


def kernel(**inputs):
    import numpy as np
    import concourse.bacc as bacc
    from concourse.bass_utils import run_bass_kernel_spmd

    a = {name: np.asarray(value) for name, value in inputs.items()}
    weights, vectors, small, hidden_bias = layout(np, a)
    consts, causal = constants(np)
    arrays = {
        "xT": np.ascontiguousarray(a["x"][0].T.reshape(DK, P, S).transpose(1, 0, 2)),
        "weights": weights, "vectors": vectors, "small": small, "hidden_bias": hidden_bias, "consts": consts, "causal": causal,
        "final_norm": np.ascontiguousarray(a["final_norm"].reshape(DK, P).T),
    }
    nc = bacc.Bacc("TRN2", target_bir_lowering=False, num_devices=1)
    args = [nc.dram_tensor(name, v.shape, mybir.dt.from_np(v.dtype), kind="ExternalInput").ap()
            for name, v in arrays.items()]
    out = nc.dram_tensor("out", (P, DK, S), F32, kind="ExternalOutput").ap()
    trunk(nc, *args, out)
    r = run_bass_kernel_spmd(nc, [arrays], core_ids=[0])
    y = r.results[0]["out"]
    return np.ascontiguousarray(y.transpose(1, 0, 2).reshape(D, S).T)[None]
```
